# Optimizing a Trainium2 kernel written in Bass

```python
import math
import jax, jax.numpy as jnp
from jax import lax
import numpy as np

D_MODEL = 1024
BATCH = 1
SEQ = 2048
DEPTH = 1

MLA_HEADS = 8
MLA_NOPE = 64
MLA_ROPE = 32
MLA_V = 64
MLA_Q_RANK = 256
MLA_KV_RANK = 128
ROPE_THETA = 10000.0
Q_BLOCK = 128
GDN_HEADS = 4
GDN_DK = 128
GDN_DV = 128
CONV_K = 4
GDN_CHUNK = 64
MLA_WIDTH = MLA_HEADS * MLA_V
GDN_WIDTH = GDN_HEADS * GDN_DV
D_MIX = MLA_WIDTH + GDN_WIDTH
GDN_QKV = 2 * GDN_HEADS * GDN_DK + GDN_HEADS * GDN_DV
IN_SPLIT_POINTS = [
    MLA_Q_RANK,
    MLA_Q_RANK + MLA_KV_RANK,
    MLA_Q_RANK + MLA_KV_RANK + MLA_ROPE,
    MLA_Q_RANK + MLA_KV_RANK + MLA_ROPE + GDN_QKV,
    MLA_Q_RANK + MLA_KV_RANK + MLA_ROPE + GDN_QKV + GDN_WIDTH,
    MLA_Q_RANK + MLA_KV_RANK + MLA_ROPE + GDN_QKV + GDN_WIDTH + GDN_HEADS,
]
D_IN = MLA_Q_RANK + MLA_KV_RANK + MLA_ROPE + GDN_QKV + GDN_WIDTH + 2 * GDN_HEADS
N_GROUPS = 4
EXPERTS_PER_GROUP = 8
N_EXPERTS = N_GROUPS * EXPERTS_PER_GROUP
TOP_K = 2
D_EXPERT = 256
MOE_BLOCK = 128
EPS = 1e-6

kernel_name = 'hybrid_mla_gdn_hmoe_adaln'

def rmsnorm(x, gain):
    xf = x.astype(jnp.float32)
    y = xf * lax.rsqrt(jnp.mean(xf * xf, axis=-1, keepdims=True) + EPS)
    return (y * gain.astype(jnp.float32)).astype(x.dtype)

def l2norm(x):
    return x * lax.rsqrt(jnp.sum(x * x, axis=-1, keepdims=True) + EPS)

def rope_tables(positions):
    inv = 1.0 / (ROPE_THETA ** (jnp.arange(0, MLA_ROPE, 2, dtype=jnp.float32) / MLA_ROPE))
    ang = positions.astype(jnp.float32)[..., None] * inv
    return jnp.cos(ang), jnp.sin(ang)

def apply_rope(t, cos, sin):
    x1, x2 = jnp.split(t.astype(jnp.float32), 2, axis=-1)
    return jnp.concatenate([x1 * cos - x2 * sin, x1 * sin + x2 * cos], axis=-1).astype(t.dtype)

def causal_mla_attention(q_nope, q_pe, k_nope, k_pe, v):
    B, S, H, _ = q_nope.shape
    nb = S // Q_BLOCK
    scale = (MLA_NOPE + MLA_ROPE) ** -0.5
    k_pos = jnp.arange(S)

    def to_blocks(t):
        return jnp.moveaxis(t.reshape((B, nb, Q_BLOCK) + t.shape[2:]), 1, 0)

    def one_block(args):
        qn, qp, i = args
        s = jnp.einsum('bqhd,bkhd->bhqk', qn, k_nope) + jnp.einsum('bqhr,bkr->bhqk', qp, k_pe)
        s = s.astype(jnp.float32) * scale
        q_pos = i * Q_BLOCK + jnp.arange(Q_BLOCK)
        s = jnp.where(k_pos[None, :] <= q_pos[:, None], s, -jnp.inf)
        p = jax.nn.softmax(s, axis=-1).astype(v.dtype)
        return jnp.einsum('bhqk,bkhd->bqhd', p, v)

    o = lax.map(one_block, (to_blocks(q_nope), to_blocks(q_pe), jnp.arange(nb)))
    return jnp.moveaxis(o, 0, 1).reshape(B, S, H, MLA_V)

def mla_mix(c_q, c_kv, k_rope, q_norm, w_uq, kv_norm, w_ukv, out_norm, cos, sin):
    B, S, _ = c_q.shape
    q = (rmsnorm(c_q, q_norm) @ w_uq).reshape(B, S, MLA_HEADS, MLA_NOPE + MLA_ROPE)
    q_nope = q[..., :MLA_NOPE]
    q_pe = apply_rope(q[..., MLA_NOPE:], cos[:, :, None, :], sin[:, :, None, :])
    kv = (rmsnorm(c_kv, kv_norm) @ w_ukv).reshape(B, S, MLA_HEADS, MLA_NOPE + MLA_V)
    k_nope, v = kv[..., :MLA_NOPE], kv[..., MLA_NOPE:]
    k_pe = apply_rope(k_rope, cos, sin)
    o = causal_mla_attention(q_nope, q_pe, k_nope, k_pe, v)
    return rmsnorm(o.reshape(B, S, MLA_WIDTH), out_norm)

def causal_depthwise_conv(x, w):
    return lax.conv_general_dilated(
        x, w[:, None, :].astype(x.dtype), window_strides=(1,), padding=((CONV_K - 1, 0),),
        dimension_numbers=('NWC', 'WIO', 'NWC'), feature_group_count=x.shape[-1])

def chunk_gated_delta_rule(q, k, v, g, beta):
    B, S, H, DK = q.shape
    DV = v.shape[-1]
    C = GDN_CHUNK
    nc = S // C

    def chunks(t):
        return jnp.moveaxis(t.reshape((B, nc, C, H) + t.shape[3:]), 3, 1)

    q, k, v, g, beta = chunks(q), chunks(k), chunks(v), chunks(g), chunks(beta)
    g = jnp.cumsum(g, axis=-1)
    idx = jnp.arange(C)
    causal = idx[:, None] >= idx[None, :]
    strict = idx[:, None] > idx[None, :]
    decay = jnp.exp(jnp.where(causal, g[..., :, None] - g[..., None, :], -jnp.inf))
    k_beta = k * beta[..., None]
    v_beta = v * beta[..., None]
    lower = jnp.where(strict, jnp.einsum('bhncd,bhnsd->bhncs', k_beta, k) * decay, 0.0)
    system = lower + jnp.eye(C, dtype=lower.dtype)
    rhs = jnp.concatenate([v_beta, k_beta * jnp.exp(g)[..., None]], axis=-1)
    sol = lax.linalg.triangular_solve(system, rhs, left_side=True, lower=True)
    u, w = sol[..., :DV], sol[..., DV:]
    a_qk = jnp.where(causal, jnp.einsum('bhncd,bhnsd->bhncs', q, k) * decay, 0.0)
    q_dec = q * jnp.exp(g)[..., None]
    g_last = g[..., -1]
    k_dec = k * jnp.exp(g_last[..., None] - g)[..., None]

    def step(state, inp):
        q_c, w_c, u_c, a_c, kd_c, gl_c = inp
        v_new = u_c - jnp.einsum('bhcd,bhde->bhce', w_c, state)
        o_c = jnp.einsum('bhcd,bhde->bhce', q_c, state) + jnp.einsum('bhcs,bhse->bhce', a_c, v_new)
        state = state * jnp.exp(gl_c)[..., None, None] + jnp.einsum('bhcd,bhce->bhde', kd_c, v_new)
        return state, o_c

    xs = tuple(jnp.moveaxis(t, 2, 0) for t in (q_dec, w, u, a_qk, k_dec, g_last))
    state0 = jnp.zeros((B, H, DK, DV), jnp.float32)
    _, o = lax.scan(step, state0, xs)
    o = jnp.moveaxis(o, 0, 2)
    return jnp.moveaxis(o, 1, 3).reshape(B, S, H, DV)

def gdn_mix(qkv, gate, a, b, conv_w, a_log, dt_bias, out_norm):
    B, S, _ = qkv.shape
    dt = qkv.dtype
    qkv = jax.nn.silu(causal_depthwise_conv(qkv, conv_w)).astype(jnp.float32)
    q, k, v = jnp.split(qkv, [GDN_HEADS * GDN_DK, 2 * GDN_HEADS * GDN_DK], axis=-1)
    q = l2norm(q.reshape(B, S, GDN_HEADS, GDN_DK)) * (GDN_DK ** -0.5)
    k = l2norm(k.reshape(B, S, GDN_HEADS, GDN_DK))
    v = v.reshape(B, S, GDN_HEADS, GDN_DV)
    g = -jnp.exp(a_log.astype(jnp.float32)) * jax.nn.softplus(a.astype(jnp.float32) + dt_bias.astype(jnp.float32))
    beta = jax.nn.sigmoid(b.astype(jnp.float32))
    o = chunk_gated_delta_rule(q, k, v, g, beta)
    o = rmsnorm(o, out_norm) * jax.nn.silu(gate.astype(jnp.float32).reshape(B, S, GDN_HEADS, GDN_DV))
    return o.reshape(B, S, GDN_WIDTH).astype(dt)

def moe_dispatch(xf, expert, gate, w1, w3, w2):
    T, D = xf.shape
    A = T * TOP_K
    nb = -(-A // MOE_BLOCK) + N_EXPERTS
    npad = nb * MOE_BLOCK
    e_flat = expert.reshape(A).astype(jnp.int32)
    tok_flat = jnp.repeat(jnp.arange(T, dtype=jnp.int32), TOP_K)
    g_flat = gate.reshape(A)
    order = jnp.argsort(e_flat)
    e_sorted = e_flat[order]
    counts = jnp.zeros((N_EXPERTS,), jnp.int32).at[e_flat].add(1)
    starts = jnp.cumsum(counts) - counts
    padded = (counts + MOE_BLOCK - 1) // MOE_BLOCK * MOE_BLOCK
    pad_ends = jnp.cumsum(padded)
    pad_starts = pad_ends - padded
    dest = pad_starts[e_sorted] + (jnp.arange(A, dtype=jnp.int32) - starts[e_sorted])
    slot_tok = jnp.full((npad,), T, jnp.int32).at[dest].set(tok_flat[order])
    slot_gate = jnp.zeros((npad,), g_flat.dtype).at[dest].set(g_flat[order])
    block_start = jnp.arange(nb, dtype=jnp.int32) * MOE_BLOCK
    block_expert = jnp.minimum(jnp.searchsorted(pad_ends, block_start, side='right'), N_EXPERTS - 1)
    x_pad = jnp.concatenate([xf, jnp.zeros((1, D), xf.dtype)], axis=0)
    xb = x_pad[slot_tok].reshape(nb, MOE_BLOCK, D)

    def expert_block(args):
        xblk, e = args
        hid = jax.nn.silu(xblk @ w1[e]) * (xblk @ w3[e])
        return hid @ w2[e]

    yb = lax.map(expert_block, (xb, block_expert)).reshape(npad, D)
    out = jnp.zeros((T + 1, D), xf.dtype).at[slot_tok].add(yb * slot_gate[:, None].astype(yb.dtype))
    return out[:T]

def hierarchical_moe(h, w_rg, b_rg, w_re, b_re, w1, w3, w2):
    B, S, D = h.shape
    T = B * S
    xf = h.reshape(T, D)
    lg = (xf @ w_rg).astype(jnp.float32) + b_rg.astype(jnp.float32)
    pg = jax.nn.softmax(lg, axis=-1)
    _, grp = lax.top_k(lg, 1)
    pg_sel = jnp.take_along_axis(pg, grp, axis=-1)
    le = ((xf @ w_re).astype(jnp.float32) + b_re.astype(jnp.float32)).reshape(T, N_GROUPS, EXPERTS_PER_GROUP)
    le = jnp.take_along_axis(le, grp[:, :, None], axis=1)[:, 0]
    top_l, top_i = lax.top_k(le, TOP_K)
    gate = pg_sel * jax.nn.softmax(top_l, axis=-1)
    expert = grp * EXPERTS_PER_GROUP + top_i
    return moe_dispatch(xf, expert, gate, w1, w3, w2).reshape(B, S, D)

def setup_inputs(seed: int = 0) -> dict:
    key = jax.random.key(seed)
    ks = jax.random.split(key, 32)
    f32 = jnp.float32
    L = DEPTH

    def nrm(k, shape, scale):
        return jax.random.normal(k, shape, f32) * scale

    def gain(k, shape):
        return 1.0 + 0.02 * jax.random.normal(k, shape, f32)

    x = nrm(ks[0], (BATCH, SEQ, D_MODEL), 1.0)
    c = nrm(ks[1], (BATCH, D_MODEL), 1.0)
    offset = jax.random.randint(ks[2], (BATCH, 1), 0, 1024, dtype=jnp.int32)
    positions = offset + jnp.arange(SEQ, dtype=jnp.int32)[None, :]
    dt0 = jnp.exp(jax.random.uniform(ks[13], (L, GDN_HEADS), f32, math.log(1e-3), math.log(1e-1)))
    return {
        'x': x,
        'c': c,
        'positions': positions,
        'w_mod': nrm(ks[3], (L, D_MODEL, 6 * D_MODEL), 0.5 * D_MODEL ** -0.5),
        'b_mod': nrm(ks[4], (L, 6 * D_MODEL), 0.02),
        'attn_norm': gain(ks[5], (L, D_MODEL)),
        'w_in': nrm(ks[6], (L, D_MODEL, D_IN), D_MODEL ** -0.5),
        'q_norm': gain(ks[7], (L, MLA_Q_RANK)),
        'w_uq': nrm(ks[8], (L, MLA_Q_RANK, MLA_HEADS * (MLA_NOPE + MLA_ROPE)), MLA_Q_RANK ** -0.5),
        'kv_norm': gain(ks[9], (L, MLA_KV_RANK)),
        'w_ukv': nrm(ks[10], (L, MLA_KV_RANK, MLA_HEADS * (MLA_NOPE + MLA_V)), MLA_KV_RANK ** -0.5),
        'conv_w': nrm(ks[11], (L, CONV_K, GDN_QKV), CONV_K ** -0.5),
        'a_log': jnp.log(jax.random.uniform(ks[12], (L, GDN_HEADS), f32, 1.0, 16.0)),
        'dt_bias': dt0 + jnp.log(-jnp.expm1(-dt0)),
        'mla_out_norm': gain(ks[14], (L, MLA_WIDTH)),
        'gdn_out_norm': gain(ks[15], (L, GDN_DV)),
        'w_out': nrm(ks[16], (L, D_MIX, D_MODEL), D_MIX ** -0.5),
        'moe_norm': gain(ks[17], (L, D_MODEL)),
        'w_route_group': nrm(ks[18], (L, D_MODEL, N_GROUPS), D_MODEL ** -0.5),
        'b_route_group': nrm(ks[19], (L, N_GROUPS), 0.01),
        'w_route_expert': nrm(ks[20], (L, D_MODEL, N_EXPERTS), D_MODEL ** -0.5),
        'b_route_expert': nrm(ks[21], (L, N_EXPERTS), 0.01),
        'w1': nrm(ks[22], (L, N_EXPERTS, D_MODEL, D_EXPERT), D_MODEL ** -0.5),
        'w3': nrm(ks[23], (L, N_EXPERTS, D_MODEL, D_EXPERT), D_MODEL ** -0.5),
        'w2': nrm(ks[24], (L, N_EXPERTS, D_EXPERT, D_MODEL), D_EXPERT ** -0.5),
        'final_norm': gain(ks[25], (D_MODEL,)),
    }

def reference(x, c, positions, w_mod, b_mod, attn_norm, w_in, q_norm, w_uq, kv_norm, w_ukv, conv_w,
              a_log, dt_bias, mla_out_norm, gdn_out_norm, w_out, moe_norm, w_route_group, b_route_group,
              w_route_expert, b_route_expert, w1, w3, w2, final_norm):
    cos, sin = rope_tables(positions)
    c_act = jax.nn.silu(c)
    for l in range(DEPTH):
        mod = c_act @ w_mod[l] + b_mod[l]
        shift_a, scale_a, gate_a, shift_m, scale_m, gate_m = jnp.split(mod[:, None, :], 6, axis=-1)
        h = rmsnorm(x, attn_norm[l]) * (1.0 + scale_a) + shift_a
        proj = h @ w_in[l]
        c_q, c_kv, k_rope, qkv, g_out, a_dec, b_beta = jnp.split(proj, IN_SPLIT_POINTS, axis=-1)
        y_mla = mla_mix(c_q, c_kv, k_rope, q_norm[l], w_uq[l], kv_norm[l], w_ukv[l], mla_out_norm[l], cos, sin)
        y_gdn = gdn_mix(qkv, g_out, a_dec, b_beta, conv_w[l], a_log[l], dt_bias[l], gdn_out_norm[l])
        x = x + gate_a * (jnp.concatenate([y_mla, y_gdn], axis=-1) @ w_out[l])
        h = rmsnorm(x, moe_norm[l]) * (1.0 + scale_m) + shift_m
        x = x + gate_m * hierarchical_moe(h, w_route_group[l], b_route_group[l], w_route_expert[l],
                                          b_route_expert[l], w1[l], w3[l], w2[l])
    return rmsnorm(x, final_norm)


_drawn_inputs = setup_inputs


def setup_inputs(seed=0):
    import zlib

    import numpy as np

    out = dict(_drawn_inputs(seed))
    spreads = {}
    factors = {'attn_norm': 7.389,
     'q_norm': 8.0,
     'kv_norm': 7.844,
     'mla_out_norm': 25.447,
     'gdn_out_norm': 8.0,
     'moe_norm': 4.714,
     'b_route_group': 8.0,
     'b_route_expert': 32.026,
     'final_norm': 7.772}
    for name, (base, spread) in spreads.items():
        noise = np.random.default_rng([zlib.crc32(name.encode()), seed]).standard_normal(out[name].shape)
        drawn = base * np.exp(spread * noise) if base else spread * noise
        out[name] = __import__('jax').numpy.asarray(drawn.astype(out[name].dtype))
    for name, factor in factors.items():
        out[name] = (out[name] * factor).astype(out[name].dtype)
    return out
```

```python
import math
from contextlib import ExitStack

import numpy as np
import concourse.bass as bass
from concourse import mybir

P = 128
F32, I32 = mybir.dt.float32, mybir.dt.int32
ALU = mybir.AluOpType
ACT = mybir.ActivationFunctionType
AX = mybir.AxisListType
ds = bass.ds

T, D = 2048, 1024
NT, ND = T // P, D // P
ST = 4
NS, SW = NT // ST, ST * P
AH, NOPE, ROPE, DV = 8, 64, 32, 64
QK = NOPE + ROPE
QR, KR = 256, 128
GH, GD = 4, 128
NC = 3 * GH
CQKV = QR + KR + ROPE
CGATE = CQKV + NC * P
CAB = CGATE + GH * GD
DIN = CAB + 2 * GH
LOWW = CQKV + 2 * GH
NG, EG = 4, 8
NE, DE = NG * EG, 256
EPS = 1e-6
HALF = ROPE // 2
NEG = -1.0e30


START = 1


def start_counts(eng, sems):
    for q in sems:
        eng.sem_inc(q, START)


def held_wait(eng, sem, value, point):
    eng.wait_ge(sem, START + value)
    eng.sem_inc(point, 1)


class Shared:
    pass


def load_w_in(sp, m, w_in):
    src = w_in[0].rearrange("(k p) n -> p k n", p=P)
    for at, first, end in ((0, 0, CQKV), (CQKV, CAB, DIN), (LOWW + NC * P, CGATE, CAB), (LOWW, CQKV, CGATE)):
        sp.dma_start(m.win[:, :, at:at + end - first], src[:, :, first:end]).then_inc(m.win_loaded, 16)


def modulation(nc, m, c, positions, w_mod, b_mod, attn_norm, w_in):
    with nc.cleanup_on_exit(), ExitStack() as ctx:
        sb = lambda n, s, d=F32: ctx.enter_context(nc.sbuf_tensor(n, s, d))
        sem = nc.alloc_semaphore
        w = [sb(f"mod_w{i}", [P, ND, D]) for i in range(2)]
        ccol, cact = sb("c_col", [P, ND]), m.c_act
        bcol, ncol = sb("b_col", [P, 2, ND]), sb("norm_col", [P, ND])
        pos_i, pos_f = sb("pos_i", [P, NT], I32), sb("pos_f", [P, NT])
        inv = sb("inv_freq", [P, HALF])
        ang, turns, red = sb("angle", [P, NT, HALF]), sb("turns", [P, NT * HALF]), sb("reduced", [P, NT * HALF])
        pcol = ctx.enter_context(nc.psum_tensor("mod_col_ps", [P, 2 * ND], F32))
        small_loaded, c_loaded = sem("small_loaded"), sem("c_loaded")
        w_loaded = [sem(f"w_loaded{i}") for i in range(2)]
        c_ready = sem("c_ready")
        w_used, col_ready = sem("w_used"), sem("col_ready")
        const_made, pool_step, dve_step = sem("const_made"), sem("pool_step"), sem("dve_step")
        inv_made, tab_reduced, tab_made = sem("inv_made"), sem("tab_reduced"), sem("tab_made")
        n_small = 3

        block = ctx.enter_context(nc.Block())

        @block.sync
        def _(sp):
            sp.dma_start(ccol[:], c.rearrange("a (p k) -> p (a k)", p=P)).then_inc(c_loaded, 16)
            for part in range(2):
                sp.dma_start(w[part][:], w_mod[0, :, part * D:(part + 1) * D]
                             .rearrange("(p k) n -> p k n", p=P)).then_inc(w_loaded[part], 16)
            load_w_in(sp, m, w_in)

        @block.gpsimd
        def _(pool):
            pool.memset(m.ident[:], 0.0).then_inc(pool_step, 1)
            pool.memset(m.ones[:], 1.0).then_inc(pool_step, 1)
            pool.memset(m.eps[:], EPS).then_inc(pool_step, 1)
            pool.memset(m.half_pow[:], -0.5).then_inc(pool_step, 1)
            pool.wait_ge(pool_step, 4)
            pool.affine_select(out=m.ident[:], in_=m.ident[:], compare_op=ALU.not_equal, fill=1.0, base=0,
                               pattern=[[-1, P]], channel_multiplier=1).then_inc(const_made, 1)
            pool.affine_select(out=m.upper[:], in_=m.ones[:], compare_op=ALU.is_ge, fill=0.0, base=0,
                               pattern=[[1, P]], channel_multiplier=-1).then_inc(const_made, 1)
            for j in range(HALF):
                f = float(np.float32(1.0) / np.float32(np.float32(10000.0) ** (np.float32(2 * j) / np.float32(ROPE))))
                pool.memset(inv[:, j:j + 1], f).then_inc(inv_made, 1)
            pool.dma_start(pos_i[:], positions.rearrange("a (n p) -> p (a n)", p=P)).then_inc(small_loaded, 16)
            pool.dma_start(ncol[:], attn_norm[0].rearrange("(k p) -> p k", p=P)).then_inc(small_loaded, 16)
            pool.dma_start(bcol[:], b_mod[0, 0:2 * D].rearrange("(a k p) -> p a k", p=P, k=ND)).then_inc(small_loaded, 16)

        @block.scalar
        def _(act):
            act.wait_ge(c_loaded, 16)
            act.activation(cact[:], ccol[:], ACT.Silu).then_inc(c_ready, 1)
            act.wait_ge(tab_reduced, 1)
            act.activation(m.cos[:], red[:], ACT.Sin).then_inc(tab_made, 1)
            act.wait_ge(tab_reduced, 2)
            act.activation(m.sin[:], ang[:].rearrange("p n j -> p (n j)"), ACT.Sin).then_inc(tab_made, 1)

        @block.tensor
        def _(pe):
            pe.wait_ge(c_ready, 1)
            for part in range(2):
                pe.wait_ge(w_loaded[part], 16)
                for j in range(ND):
                    for k in range(ND):
                        last = pe.matmul(pcol[:, part * ND + j:part * ND + j + 1], w[part][:, k, j * P:(j + 1) * P],
                                         cact[:, k:k + 1], start=(k == 0), stop=(k == ND - 1))
                last.then_inc(w_used, 1)

        @block.vector
        def _(dve):
            dve.wait_ge(small_loaded, 16 * n_small)
            n = [0]

            def step(ins):
                n[0] += 1
                ins.then_inc(dve_step, 1)
                dve.wait_ge(dve_step, n[0])

            step(dve.tensor_copy(pos_f[:], pos_i[:]))
            dve.wait_ge(inv_made, HALF)
            step(dve.tensor_tensor(ang[:], pos_f[:].unsqueeze(2).to_broadcast([P, NT, HALF]),
                                   inv[:].unsqueeze(1).to_broadcast([P, NT, HALF]), ALU.mult))
            flat = ang[:].rearrange("p n j -> p (n j)")
            c1 = 6.28125
            c2 = round((2 * math.pi - c1) * 2 ** 21) / 2 ** 21
            c3 = 2 * math.pi - c1 - c2
            magic = float(1.5 * 2 ** 23)
            lim = 3.1415925

            def reduce_to(dst, quarter):
                step(dve.tensor_scalar(turns[:], flat, 1 / (2 * math.pi), quarter / 4, ALU.mult, ALU.add))
                step(dve.tensor_scalar(turns[:], turns[:], magic, None, ALU.add))
                step(dve.tensor_scalar(turns[:], turns[:], magic, None, ALU.subtract))
                src = flat
                for cc in (c1, c2, c3):
                    step(dve.scalar_tensor_tensor(out=dst, in0=turns[:], scalar=-cc, in1=src, op0=ALU.mult, op1=ALU.add))
                    src = dst
                step(dve.tensor_scalar(dst, dst, quarter * math.pi / 2, lim, ALU.add, ALU.min))
                dve.tensor_scalar(dst, dst, -lim, None, ALU.max).then_inc(tab_reduced, 1)

            reduce_to(red[:], 1)
            reduce_to(flat, 0)
            dve.wait_ge(w_used, 2)
            dve.tensor_tensor(m.shift_a[:], pcol[:, 0:ND], bcol[:, 0, :], ALU.add).then_inc(col_ready, 1)
            step(dve.tensor_tensor(bcol[:, 1, :], pcol[:, ND:2 * ND], bcol[:, 1, :], ALU.add))
            dve.scalar_tensor_tensor(out=m.gain_a[:], in0=bcol[:, 1, :], scalar=1.0, in1=ncol[:],
                                     op0=ALU.add, op1=ALU.mult).then_inc(col_ready, 1)
            dve.wait_ge(const_made, 2)
            dve.wait_ge(tab_made, 2)


def projection(nc, m, x, q_norm, w_uq, kv_norm, w_ukv, conv_w):
    order = [("T", t) for t in range(ST)]
    for t in range(ST):
        v = 3 * t
        order += [("P", t)] + ([("HK", t - 1)] if t else []) + [("V", v)]
        if t < 3:
            order += ([("S", v - 1)] if v else []) + [("C", t), ("V", v + 1), ("S", v), ("Q", t), ("V", v + 2),
                                                      ("S", v + 1), ("K", t), ("HQ", t)]
        else:
            order += [("S", 8), ("C", t), ("SQ", 0), ("SQ", 1), ("L", 0), ("SQ", 2), ("L", 1), ("V", 10), ("SQ", 3),
                      ("L", 2), ("SQ", 4), ("L", 3), ("Q", t), ("SQ", 5), ("L", 4), ("SQ", 6), ("L", 5),
                      ("SQ", 7), ("L", 6), ("L", 7), ("S", 9), ("K", t), ("V", 11), ("HQ", t), ("S", 10), ("S", 11),
                      ("HK", t)]
    NL = 2 * GH
    with nc.cleanup_on_exit(), ExitStack() as ctx:
        sb = lambda n, s, d=F32: ctx.enter_context(nc.sbuf_tensor(n, s, d))
        ps = lambda n, s: ctx.enter_context(nc.psum_tensor(n, s, F32))
        sems = []

        def sem(name):
            sems.append(nc.alloc_semaphore(name))
            return sems[-1]

        win = m.win
        QKV0, GATE0 = LOWW, LOWW + NC * P
        wuq, wukv = sb("w_uq_sb", [P, 2, AH * QK]), sb("w_ukv_sb", [P, AH * (NOPE + DV)])
        lat_gain = sb("latent_gain", [P, 3])
        taps = sb("conv_taps", [P, NC, 4])
        xin, xn = sb("x_in", [P, 2, D]), sb("x_normed", [P, D])
        junk = sb("square_junk", [P, D])
        ss, ms, rs = sb("x_sumsq", [P, 2]), sb("x_meansq", [P, 2]), sb("x_rstd", [P, 2])
        hT = sb("h_transposed", [P, ND, SW])
        low = sb("low", [P, LOWW])
        gate = sb("gate_out", [P, GH * GD])
        cs, cm, cr, cinv = (sb(n, [P, 2]) for n in ("lat_sumsq", "lat_meansq", "lat_rstd", "lat_inv"))
        cn, cT = sb("lat_normed", [P, 3 * P]), sb("lat_transposed", [P, 3 * P])
        qtok = sb("q_and_key_rope_tok", [P, AH + 1, QK])
        ktok = sb("k_tok", [P, AH, QK])
        rin, prod = sb("rope_in", [P, AH + 1, ROPE]), sb("rope_products", [P, 4, AH + 1, HALF])
        vsb = sb("v_tok", [P, AH, DV])
        qTs, kTs = sb("qT_out", [QK, AH, P]), sb("kT_out", [QK, AH, P])
        raw = sb("conv_in", [P, 2, SW + 3])
        halo = sb("conv_halo", [P, NC, 3])
        acc = sb("conv_acc", [P, 2, SW])
        sil = sb("silu_out", [P, NL, SW])
        vT = sb("vT_out", [P, 2, SW])
        sq, lnb, rn, nrm = sb("l2_square", [P, 2, SW]), sb("l2_ln", [P, SW]), sb("l2_rstd", [P, SW]), sb("l2_out", [P, 2, SW])
        qbias = sb("l2_bias", [P, 2])
        pT, pQ = ps("pT", [P, 2, 512]), ps("pQ", [P, 2, 512])
        pA, pG = ps("pA", [P, 512]), ps("pG", [P, 512])
        pV = [ps(f"pV{i}", [P, 512]) for i in range(2)]

        w_loaded, n_weights = sem("w_loaded"), 8
        x_loaded = [sem(f"x_loaded{i}") for i in range(2)]
        w_scaled, halo_zero, const_set, wait_point = sem("w_scaled"), sem("halo_zero"), sem("const_set"), sem("wait_point")
        x_squared, ms_ready, eps_added, rstd_ready = sem("x_squared"), sem("ms_ready"), sem("eps_added"), sem("rstd_ready")
        xn_written = sem("xn_written")
        xT_ready, hT_act, hT_dve = sem("xT_ready"), sem("hT_act"), sem("hT_dve")
        low_ready, low_copied, gate_done, gate_stored = sem("low_ready"), sem("low_copied"), sem("gate_done"), sem("gate_stored")
        lat_squared, lat_step, lat_normed = sem("lat_squared"), sem("lat_step"), sem("lat_normed")
        latT_ready, latT_copied = sem("latT_ready"), sem("latT_copied")
        q_ready, q_copied, rope_prod, rope_done = sem("q_ready"), sem("q_copied"), sem("rope_prod"), sem("rope_done")
        kv_ready, kn_copied, v_copied, kpe_copied, v_stored = (
            sem("kv_ready"), sem("kn_copied"), sem("v_copied"), sem("kpe_copied"), sem("v_stored"))
        qT_ready, qT_act, qT_dve, qT_stored = sem("qT_ready"), sem("qT_act"), sem("qT_dve"), sem("qT_stored")
        kT_ready, kT_act, kT_dve, kT_stored = sem("kT_ready"), sem("kT_act"), sem("kT_dve"), sem("kT_stored")
        conv_proj = sem("conv_proj")
        raw_written, conv_done, silu_done = sem("raw_written"), sem("conv_done"), sem("silu_done")
        halo_in, halo_out, conv_step = sem("halo_in"), sem("halo_out"), sem("conv_step")
        sq_done, l2_sum, ln_done, rn_done, l2_done = sem("sq_done"), sem("l2_sum"), sem("ln_done"), sem("rn_done"), sem("l2_done")
        out_stored = [sem(f"qkv_stored{i}") for i in range(2)]
        vt_stored = [sem(f"vT_stored{i}") for i in range(2)]
    
        block = ctx.enter_context(nc.Block())

        @block.sync
        def _(sp):
            start_counts(sp, sems[0::5])
            sp.dma_start(lat_gain[:, 0:2], q_norm[0].rearrange("(k p) -> p k", p=P)).then_inc(w_loaded, 16)
            sp.dma_start(lat_gain[:, 2:3], kv_norm[0].rearrange("(k p) -> p k", p=P)).then_inc(w_loaded, 16)
            for t in range(2):
                sp.dma_start(xin[:, t, :], x[0, t * P:(t + 1) * P, :]).then_inc(x_loaded[t], 16)
            sp.dma_start(wuq[:], w_uq[0].rearrange("(k p) n -> p k n", p=P)).then_inc(w_loaded, 16)
            sp.dma_start(wukv[:], w_ukv[0]).then_inc(w_loaded, 16)
            for j in range(4):
                sp.dma_start(taps[:, :, j], conv_w[0, j].rearrange("(c p) -> p c", p=P)).then_inc(w_loaded, 16)
            with sp.Fori(0, NS) as s:

                def load_x(ahead):
                    held_wait(sp, xn_written, s * ST + ahead + 1, wait_point)
                    sp.dma_start(xin[:, ahead % 2, :], x[0, ds(((s * ST + ahead) % NT) * P, P), :]
                                 ).then_inc(x_loaded[ahead % 2], 16)

                for kind, n in order:
                    tile = s * ST + n
                    if kind == "T" and n < 2:
                        load_x(n + 2)
                    elif kind == "P":
                        held_wait(sp, gate_done, s * ST + n + 1, wait_point)
                        sp.dma_start(m.gate_d[ds(tile * P, P), :], gate[:]).then_inc(gate_stored, 16)
                    elif kind == "K":
                        held_wait(sp, v_copied, s * ST + n + 1, wait_point)
                        sp.dma_start(m.v_d[ds(tile * P, P), :], vsb[:].rearrange("p h d -> p (h d)")).then_inc(v_stored, 16)
                    elif kind == "HQ":
                        held_wait(sp, qT_act, s * ST + n + 1, wait_point)
                        held_wait(sp, qT_dve, s * ST + n + 1, wait_point)
                        sp.dma_start(m.qT_d[ds(tile * QK, QK), :], qTs[:].rearrange("p h d -> p (h d)")).then_inc(qT_stored, 16)
                        if n == 2:
                            load_x(4)
                            load_x(5)
                    elif kind == "HK":
                        held_wait(sp, kT_act, s * ST + n + 1, wait_point)
                        held_wait(sp, kT_dve, s * ST + n + 1, wait_point)
                        sp.dma_start(m.kT_d[ds(tile * QK, QK), :], kTs[:].rearrange("p h d -> p (h d)")).then_inc(kT_stored, 16)
                    elif kind in ("S", "L") and (kind == "L" or n >= NL):
                        if kind == "L":
                            held_wait(sp, l2_done, s * NL + n + 1, wait_point)
                            src, done = nrm[:, n % 2, :], out_stored[n % 2]
                            slot = 2 * n + 1 if n < GH else 2 * (n - GH)
                        else:
                            held_wait(sp, silu_done, s * NC + n + 1 + 2, wait_point)
                            src, done, slot = vT[:, n % 2, :], vt_stored[n % 2], n
                        sp.dma_start(m.qkv_d[ds(s * ST, ST), :, slot, :].rearrange("t p i -> p t i"),
                                     src.rearrange("p (t i) -> p t i", t=ST)).then_inc(done, 16)
            for q in (gate_stored, v_stored, qT_stored, kT_stored):
                sp.wait_ge(q, START + 16 * NT)
            for i in range(2):
                sp.wait_ge(out_stored[i], START + 16 * NS * NL // 2)
                sp.wait_ge(vt_stored[i], START + 16 * NS * GH // 2)
                sp.wait_ge(x_loaded[i], START + 16 * (NT // 2 + 1))

        @block.gpsimd
        def _(pool):
            start_counts(pool, sems[1::5])
            pool.memset(halo[:], 0.0).then_inc(halo_zero, 1)
            pool.memset(cinv[:, 0:1], 1.0 / QR).then_inc(const_set, 1)
            pool.memset(cinv[:, 1:2], 1.0 / KR).then_inc(const_set, 1)
            pool.memset(qbias[:, 0:1], -0.5 * math.log(GD)).then_inc(const_set, 1)
            pool.memset(qbias[:, 1:2], 0.0).then_inc(const_set, 1)
            pool.wait_ge(halo_zero, START + 1)
            pool.wait_ge(const_set, START + 4)
            with pool.Fori(0, NS) as s:

                def wait(q, v):
                    held_wait(pool, q, v, wait_point)

                for kind, n in order:
                    if kind == "T":
                        p = n % 2
                        wait(x_squared, s * ST + n + 1)
                        pool.tensor_scalar(ms[:, p:p + 1], ss[:, p:p + 1], 1.0 / D, EPS, ALU.mult, ALU.add).then_inc(ms_ready, 1)
                        wait(ms_ready, s * ST + n + 1)
                        pool.tensor_tensor(rs[:, p:p + 1], ms[:, p:p + 1], m.half_pow[:, 0:1], ALU.pow).then_inc(rstd_ready, 1)
                    elif kind == "P":
                        wait(lat_squared, (s * ST + n) * 2 + 2)
                        for i in range(3):
                            if i:
                                wait(lat_step, (s * ST + n) * 3 + i)
                            if i == 0:
                                ins = pool.tensor_tensor(cm[:], cs[:], cinv[:], ALU.mult)
                            elif i == 1:
                                ins = pool.tensor_scalar(cm[:], cm[:], EPS, None, ALU.add)
                            else:
                                ins = pool.tensor_tensor(cr[:], cm[:], m.half_pow[:, 0:2], ALU.pow)
                            ins.then_inc(lat_step, 1)
                    elif kind == "K":
                        wait(rope_done, (s * ST + n) * 2 + 2)
                        wait(kT_ready, s * ST + n)
                        pool.tensor_copy(ktok[:, :, NOPE:], qtok[:, AH, NOPE:].unsqueeze(1).to_broadcast([P, AH, ROPE])
                                         ).then_inc(kpe_copied, 1)
                    elif kind == "V":
                        i = s * NC + n
                        wait(conv_done, i + 1)
                        wait(halo_out, s * NC + n)
                        pool.tensor_copy(raw[:, n % 2, 0:3], halo[:, n, :]).then_inc(halo_in, 1)
                        wait(raw_written, i + 1 + 2)
                        wait(halo_in, i + 1)
                        pool.tensor_copy(halo[:, n, :], raw[:, n % 2, SW:SW + 3]).then_inc(halo_out, 1)

        @block.scalar
        def _(act):
            start_counts(act, sems[2::5])
            act.sem_inc(raw_written, 2)
            act.sem_inc(silu_done, 2)
            act.wait_ge(w_loaded, START + 16 * n_weights)
            for k in range(2):
                act.activation(wuq[:, k, :], wuq[:, k, :], ACT.Copy, scale=lat_gain[:, k:k + 1]).then_inc(w_scaled, 1)
            act.activation(wukv[:], wukv[:], ACT.Copy, scale=lat_gain[:, 2:3]).then_inc(w_scaled, 1)
            act.wait_ge(const_set, START + 4)
            with act.Fori(0, NS) as s:
                for kind, n in order:
                    i = s * ST + n
                    if kind == "T":
                        act.wait_ge(x_loaded[n % 2], START + (s * 2 + n // 2 + 1) * 16)
                        act.wait_ge(rstd_ready, START + i)
                        act.activation(junk[:], xin[:, n % 2, :], ACT.Square, accum_out=ss[:, n % 2:n % 2 + 1]
                                       ).then_inc(x_squared, 1)
                        act.wait_ge(xT_ready, START + i + 1)
                        act.wait_ge(conv_proj, START + s * NC)
                        for k in range(ND // 2):
                            last = act.activation(hT[:, k, n * P:(n + 1) * P], pT[:, 0, k * P:(k + 1) * P], ACT.Identity,
                                                  scale=m.gain_a[:, k:k + 1], bias=m.shift_a[:, k:k + 1])
                        last.then_inc(hT_act, 1)
                    elif kind == "P":
                        act.wait_ge(low_copied, START + i + 1)
                        act.wait_ge(lat_step, START + i * 3)
                        act.activation(junk[:, 0:QR], low[:, 0:QR], ACT.Square, accum_out=cs[:, 0:1]).then_inc(lat_squared, 1)
                        act.activation(junk[:, QR:QR + KR], low[:, QR:QR + KR], ACT.Square, accum_out=cs[:, 1:2]
                                       ).then_inc(lat_squared, 1)
                        act.wait_ge(gate_stored, START + i * 16)
                        act.activation(gate[:], pG[:], ACT.Silu).then_inc(gate_done, 1)
                    elif kind == "C":
                        act.wait_ge(latT_ready, START + i + 1)
                        act.wait_ge(kv_ready, START + i)
                        act.copy(cT[:], pT[:, 0, 0:3 * P]).then_inc(latT_copied, 1)
                    elif kind == "Q":
                        act.wait_ge(q_ready, START + i + 1)
                        act.wait_ge(qT_ready, START + i)
                        q4 = pQ[:, :, 0:4 * QK].rearrange("p b (h d) -> p b h d", h=4)
                        act.copy(qtok[:, 0:AH, 0:NOPE].rearrange("p (b h) d -> p b h d", b=2), q4[:, :, :, 0:NOPE])
                        act.wait_ge(rope_prod, START + i * 4)
                        act.copy(rin[:, 0:AH, :].rearrange("p (b h) d -> p b h d", b=2), q4[:, :, :, NOPE:])
                        act.wait_ge(low_copied, START + i + 1)
                        act.copy(rin[:, AH, :], low[:, QR + KR:CQKV]).then_inc(q_copied, 1)
                    elif kind == "K":
                        act.wait_ge(kv_ready, START + i + 1)
                        act.wait_ge(kT_ready, START + i)
                        act.copy(ktok[:, :, 0:NOPE], pQ[:].rearrange("p b (h d) -> p (b h) d", h=4)[:, :, 0:NOPE]
                                 ).then_inc(kn_copied, 1)
                    elif kind in ("HQ", "HK"):
                        ready, stored, dst, done = (qT_ready, qT_stored, qTs, qT_act) if kind == "HQ" else (
                            kT_ready, kT_stored, kTs, kT_act)
                        act.wait_ge(ready, START + i + 1)
                        act.wait_ge(stored, START + i * 16)
                        act.copy(dst[:, 0:4, :], pT[0:QK, 0, :].rearrange("p (h t) -> p h t", h=4)).then_inc(done, 1)
                    elif kind == "V":
                        v = s * NC + n
                        act.wait_ge(conv_proj, START + v + 1)
                        act.wait_ge(conv_done, START + v + 1)
                        act.wait_ge(halo_out, START + v)
                        act.copy(raw[:, n % 2, 3:], pV[n % 2][:]).then_inc(raw_written, 1)
                    elif kind == "S":
                        v = s * NC + n
                        act.wait_ge(conv_done, START + v + 1 + 2)
                        if n < NL:
                            act.wait_ge(l2_done, START + s * NL)
                            dst = sil[:, n, :]
                        else:
                            act.wait_ge(vt_stored[n % 2], START + (s * 2 + (n - NL) // 2) * 16)
                            dst = vT[:, n % 2, :]
                        act.activation(dst, acc[:, n % 2, :], ACT.Silu).then_inc(silu_done, 1)
                    elif kind == "SQ":
                        j = s * NL + n
                        if n == 0:
                            act.preload_act_table_set("natural_log_exp_and_others")
                        act.wait_ge(silu_done, START + s * NC + n + 1 + 2)
                        if n >= 2:
                            act.wait_ge(l2_sum, START + j - 1)
                        else:
                            act.wait_ge(l2_sum, START + s * NL)
                        act.activation(sq[:, n % 2, :], sil[:, n, :], ACT.Square).then_inc(sq_done, 1)
                    elif kind == "L":
                        j = s * NL + n
                        act.wait_ge(l2_sum, START + j + 1)
                        act.wait_ge(rn_done, START + j)
                        act.activation(lnb[:], pT[:, n % 2, :], ACT.Ln, bias=m.eps[:, 0:1]).then_inc(ln_done, 1)
                        act.wait_ge(ln_done, START + j + 1)
                        act.wait_ge(l2_done, START + j)
                        q = 0 if n < GH else 1
                        act.activation(rn[:], lnb[:], ACT.Exp, scale=-0.5, bias=qbias[:, q:q + 1]).then_inc(rn_done, 1)

        @block.vector
        def _(dve):
            start_counts(dve, sems[3::5])
            dve.sem_inc(xn_written, 2)
            dve.sem_inc(conv_done, 2)
            dve.wait_ge(w_loaded, START + 16 * n_weights)
            with dve.Fori(0, NS) as s:
                for kind, n in order:
                    i = s * ST + n
                    if kind == "T":
                        dve.wait_ge(rstd_ready, START + i + 1)
                        dve.wait_ge(xT_ready, START + i)
                        dve.tensor_scalar(xn[:], xin[:, n % 2, :], rs[:, n % 2:n % 2 + 1], None, ALU.mult).then_inc(xn_written, 1)
                        dve.wait_ge(xT_ready, START + i + 1)
                        dve.wait_ge(conv_proj, START + s * NC)
                        for k in range(ND // 2, ND):
                            last = dve.tensor_scalar(hT[:, k, n * P:(n + 1) * P], pT[:, 1, (k - 4) * P:(k - 3) * P],
                                                     m.gain_a[:, k:k + 1], m.shift_a[:, k:k + 1], ALU.mult, ALU.add)
                        last.then_inc(hT_dve, 1)
                    elif kind == "P":
                        dve.wait_ge(low_ready, START + i + 1)
                        dve.wait_ge(q_copied, START + i)
                        dve.wait_ge(lat_squared, START + i * 2)
                        dve.tensor_copy(low[:], pA[:, 0:LOWW])
                        dve.tensor_copy(m.ab[:, ds(i * 2 * GH, 2 * GH)], pA[:, CQKV:LOWW]).then_inc(low_copied, 1)
                        dve.wait_ge(low_copied, START + i + 1)
                        dve.wait_ge(lat_step, START + i * 3 + 3)
                        dve.wait_ge(latT_ready, START + i)
                        dve.tensor_scalar(cn[:, 0:QR], low[:, 0:QR], cr[:, 0:1], None, ALU.mult)
                        dve.tensor_scalar(cn[:, QR:], low[:, QR:QR + KR], cr[:, 1:2], None, ALU.mult).then_inc(lat_normed, 1)
                    elif kind == "Q":
                        dve.wait_ge(q_copied, START + i + 1)
                        dve.wait_ge(rope_done, START + i * 2)
                        halves = (rin[:, :, 0:HALF], rin[:, :, HALF:])
                        for j, (half, tab) in enumerate(((0, m.cos), (1, m.sin), (0, m.sin), (1, m.cos))):
                            row = tab[:, ds(i * HALF, HALF)].unsqueeze(1).to_broadcast([P, AH + 1, HALF])
                            dve.tensor_tensor(prod[:, j], halves[half], row, ALU.mult).then_inc(rope_prod, 1)
                        dve.wait_ge(rope_prod, START + i * 4 + 4)
                        dve.wait_ge(qT_ready, START + i)
                        dve.wait_ge(kpe_copied, START + i)
                        dve.tensor_tensor(qtok[:, :, NOPE:NOPE + HALF], prod[:, 0], prod[:, 1], ALU.subtract).then_inc(rope_done, 1)
                        dve.tensor_tensor(qtok[:, :, NOPE + HALF:], prod[:, 2], prod[:, 3], ALU.add).then_inc(rope_done, 1)
                    elif kind == "K":
                        dve.wait_ge(kn_copied, START + i + 1)
                        dve.wait_ge(v_stored, START + i * 16)
                        dve.tensor_copy(vsb[:], pQ[:].rearrange("p b (h d) -> p (b h) d", h=4)[:, :, NOPE:]).then_inc(v_copied, 1)
                    elif kind in ("HQ", "HK"):
                        ready, stored, dst, done = (qT_ready, qT_stored, qTs, qT_dve) if kind == "HQ" else (
                            kT_ready, kT_stored, kTs, kT_dve)
                        dve.wait_ge(ready, START + i + 1)
                        dve.wait_ge(stored, START + i * 16)
                        dve.tensor_copy(dst[:, 4:8, :], pT[0:QK, 1, :].rearrange("p (h t) -> p h t", h=4)).then_inc(done, 1)
                    elif kind == "V":
                        v, b = s * NC + n, n % 2
                        dve.wait_ge(raw_written, START + v + 1 + 2)
                        dve.wait_ge(halo_in, START + v + 1)
                        dve.wait_ge(silu_done, START + v + 1)
                        dve.tensor_scalar(acc[:, b, :], raw[:, b, 3:], taps[:, n, 3:4], None, ALU.mult).then_inc(conv_step, 1)
                        for j in (2, 1, 0):
                            dve.wait_ge(conv_step, START + v * 3 + 3 - j)
                            dve.scalar_tensor_tensor(out=acc[:, b, :], in0=raw[:, b, j:j + SW], scalar=taps[:, n, j:j + 1],
                                                     in1=acc[:, b, :], op0=ALU.mult, op1=ALU.add
                                                     ).then_inc(conv_step if j else conv_done, 1)
                    elif kind == "L":
                        j = s * NL + n
                        dve.wait_ge(rn_done, START + j + 1)
                        dve.wait_ge(out_stored[n % 2], START + (s * (NL // 2) + n // 2) * 16)
                        dve.tensor_tensor(nrm[:, n % 2, :], sil[:, n, :], rn[:], ALU.mult).then_inc(l2_done, 1)

        @block.tensor
        def _(pe):
            start_counts(pe, sems[4::5])
            pe.wait_ge(w_loaded, START + 16 * n_weights)
            pe.wait_ge(w_scaled, START + 3)
            pe.wait_ge(m.win_loaded, 16 * 4)
            with pe.Fori(0, NS) as s:
                pT_read = [(kT_act, s * ST), (kT_dve, s * ST)]
                l_read = {}
                for kind, n in order:
                    i = s * ST + n
                    if kind == "T":
                        pe.wait_ge(xn_written, START + i + 1 + 2)
                        for q, v in pT_read:
                            pe.wait_ge(q, START + v)
                        for k in range(ND):
                            last = pe.transpose(pT[:, k // 4, (k % 4) * P:(k % 4 + 1) * P], xn[:, k * P:(k + 1) * P], m.ident[:])
                        last.then_inc(xT_ready, 1)
                        pT_read = [(hT_act, i + 1), (hT_dve, i + 1)]
                    elif kind == "P":
                        if n == 0:
                            pe.wait_ge(hT_act, START + s * ST + ST)
                            pe.wait_ge(hT_dve, START + s * ST + ST)
                        pe.wait_ge(low_copied, START + i)
                        pe.wait_ge(gate_done, START + i)
                        for k in range(ND):
                            lhs = hT[:, k, n * P:(n + 1) * P]
                            pe.matmul(pA[:, 0:LOWW], lhs, win[:, k, 0:LOWW], start=(k == 0), stop=(k == ND - 1))
                            last = pe.matmul(pG[:], lhs, win[:, k, GATE0:], start=(k == 0), stop=(k == ND - 1))
                        last.then_inc(low_ready, 1)
                    elif kind == "C":
                        pe.wait_ge(lat_normed, START + i + 1)
                        for q, v in pT_read:
                            pe.wait_ge(q, START + v)
                        for k in range(3):
                            last = pe.transpose(pT[:, 0, k * P:(k + 1) * P], cn[:, k * P:(k + 1) * P], m.ident[:])
                        last.then_inc(latT_ready, 1)
                        pT_read = [(latT_copied, i + 1)]
                    elif kind == "Q":
                        pe.wait_ge(latT_copied, START + i + 1)
                        pe.wait_ge(kn_copied, START + i)
                        pe.wait_ge(v_copied, START + i)
                        for b in range(2):
                            for k in range(2):
                                last = pe.matmul(pQ[:, b, 0:4 * QK], cT[:, k * P:(k + 1) * P],
                                                 wuq[:, k, b * 4 * QK:(b + 1) * 4 * QK], start=(k == 0), stop=(k == 1))
                        last.then_inc(q_ready, 1)
                    elif kind == "K":
                        pe.wait_ge(q_copied, START + i + 1)
                        for b in range(2):
                            last = pe.matmul(pQ[:, b, :], cT[:, QR:], wukv[:, b * 512:(b + 1) * 512], start=True, stop=True)
                        last.then_inc(kv_ready, 1)
                    elif kind in ("HQ", "HK"):
                        if kind == "HQ":
                            pe.wait_ge(rope_done, START + i * 2 + 2)
                        else:
                            pe.wait_ge(kn_copied, START + i + 1)
                            pe.wait_ge(kpe_copied, START + i + 1)
                        for q, v in pT_read:
                            pe.wait_ge(q, START + v)
                        src = qtok if kind == "HQ" else ktok
                        for h in range(AH):
                            last = pe.transpose(pT[0:QK, h // 4, (h % 4) * P:(h % 4 + 1) * P], src[:, h, :], m.ident[:])
                        last.then_inc(qT_ready if kind == "HQ" else kT_ready, 1)
                        pT_read = [(qT_act, i + 1), (qT_dve, i + 1)] if kind == "HQ" else [(kT_act, i + 1), (kT_dve, i + 1)]
                    elif kind == "V":
                        pe.wait_ge(raw_written, START + s * NC + n + 1)
                        for k in range(ND):
                            last = pe.matmul(pV[n % 2][:], win[:, k, QKV0 + n * P:QKV0 + (n + 1) * P], hT[:, k, :],
                                             start=(k == 0), stop=(k == ND - 1))
                        last.then_inc(conv_proj, 1)
                    elif kind == "L":
                        j = s * NL + n
                        pe.wait_ge(sq_done, START + j + 1)
                        if n < 2:
                            for q, v in pT_read:
                                pe.wait_ge(q, START + v)
                        else:
                            pe.wait_ge(ln_done, START + j - 1)
                        pe.matmul(pT[:, n % 2, :], m.ones[:], sq[:, n % 2, :], start=True, stop=True).then_inc(l2_sum, 1)
                        if n == NL - 1:
                            pT_read = [(ln_done, j + 1)]


def delta(nc, m, a_log, dt_bias, w_mod, b_mod):
    LV = 7
    H2 = GH // 2
    order = ["K", "VT", "KD", "LT", "U0", "W0", "KS", ("N", 1), "TR", "UTA", ("M", 0), ("N", 2), "VN", ("M", 1),
             ("N", 3), "AV", "G", ("M", 2), ("N", 4), "O1", ("M", 3), ("N", 5), "O2", ("N", 6)]
    NM = sum(s[0] == "M" for s in order)
    MW = 4 * D // (2 * NM)
    with nc.cleanup_on_exit(), ExitStack() as ctx:
        sb = lambda n, s, d=F32: ctx.enter_context(nc.sbuf_tensor(n, s, d))
        ps = lambda n, s: ctx.enter_context(nc.psum_tensor(n, s, F32))
        sems = []

        def sem(name):
            sems.append(nc.alloc_semaphore(name))
            return sems[-1]

        alog, dtb = sb("a_log_row", [P, GH]), sb("dt_row", [P, GH])
        xs, absx, bcl, sp_ = (sb(n, [P, NT, GH]) for n in ("dec_x", "dec_abs", "beta_in", "softplus"))
        alpha, beta, gcol = (sb(n, [P, NT * GH]) for n in ("alpha", "beta", "g_cum"))
        eg, neg_eg, etot, ekd = (sb(n, [P, NT * GH]) for n in ("exp_g", "neg_exp_g", "exp_total", "exp_to_end"))
        masks = sb("level_masks", [P, LV, P])
        kq = [sb(f"kqv{i}", [P, NC, P]) for i in range(2)]
        gate = sb("gate_in", [P, 2, GH, GD])
        uta, dm, em = sb("decayed_upper", [P, GH, P]), sb("g_diff", [P, GH, P]), sb("decay", [P, GH, P])
        lt = sb("A_transposed", [P, GH, P])
        xt = sb("X_transposed", [P, LV, GH, P])
        U = [sb(f"U{i}", [P, GH, P]) for i in range(2)]
        at = [sb(f"qk_transposed{i}", [P, GH, P]) for i in range(2)]
        W = [sb(f"W_g{g}", [P, H2, P]) for g in range(2)]
        Y = [sb(f"Y_g{g}", [P, H2, P]) for g in range(2)]
        vtok, kd, R, qs, vn = (sb(n, [P, GH, P]) for n in ("v_chunk", "k_to_end", "residual", "q_state", "v_new"))
        S = sb("state", [P, GH, P])
        o, osq, y = sb("o_chunk", [P, GH, P]), sb("o_square", [P, GH, P]), sb("y_chunk", [P, GH, P])
        oss, oms, orr = sb("o_sumsq", [P, GH]), sb("o_meansq", [P, GH]), sb("o_rstd", [P, GH])
        modw, mod_part = sb("w_mod_rows", [P, 4 * D]), sb("mod_part", [P, MW])
        mod_rows = m.mod_rows[:].rearrange("p a n -> p (a n)")
        bA, bB, bC, bD = (ps(f"bank{n}", [P, GH, P]) for n in "ABCD")
        bY = [ps(f"bankY{g}", [P, H2, P]) for g in range(2)]
        bW = [ps(f"bankW{g}", [P, 2, H2, P]) for g in range(2)]

        pre, rows_loaded, mask_step, state_zero, wait_point = (
            sem("pre"), sem("rows_loaded"), sem("mask_step"), sem("state_zero"), sem("wait_point2"))
        kq_loaded, gate_loaded = [sem(f"kq_loaded{i}") for i in range(2)], [sem(f"gate_loaded{i}") for i in range(2)]
        uta_ready, grow_ready, dm_ready, dm_clamped, exp_ready, em_ready = (sem(n) for n in (
            "uta_ready", "grow_ready", "dm_ready", "dm_clamped", "exp_ready", "em_ready"))
        kk_ready, lt_ready, at_ready, xt_ready, u0_ready, w0_ready, w0_copied = (sem(n) for n in (
            "kk_ready", "lt_ready", "at_ready", "xt_ready", "u0_ready", "w0_ready", "w0_copied"))
        vt_ready, v_copied, kt_ready, kd_ready = sem("vt_ready"), sem("v_copied2"), sem("kt_ready"), sem("kd_ready")
        ks_ready, r_ready, qs_ready, tr_ready, vn_ready = (sem(n) for n in (
            "ks_ready", "r_ready", "qs_ready", "tr_ready", "vn_ready"))
        av_ready, ds_ready, state_ready, o_ready, osq_ready, oss_ready, o_pow, y_ready = (sem(n) for n in (
            "av_ready", "ds_ready", "state_ready", "o_ready", "osq_ready", "oss_ready", "o_pow", "y_ready"))
        y_stored = sem("y_stored")
        rows_zero, bias_loaded = nc.alloc_semaphore("rows_zero"), nc.alloc_semaphore("bias_loaded")
        modw_loaded, mod_scaled, mod_added = (sem(n) for n in (
            "modw_loaded", "mod_scaled", "mod_added"))
        xw_ready, y_copied = [sem(f"xw_ready{g}") for g in range(2)], [sem(f"y_copied{g}") for g in range(2)]
        wy_ready, uw_updated = [sem(f"wy_ready{g}") for g in range(2)], [sem(f"uw_updated{g}") for g in range(2)]
        NLV = LV - 1

        def steps(body, eng):
            body(-2, 0, (False, False, True), 0)
            body(-1, 1, (True, False, True), 0)
            with eng.Fori(0, NT // 2 - 1) as i:
                body(i * 2, 0, (True, True, True), i)
                body(i * 2 + 1, 1, (True, True, True), i)
            body(NT - 2, 0, (True, True, False), NT // 2 - 1)
            body(NT - 1, 1, (False, True, False), NT // 2 - 1)

        def parts(does):
            prep, rec, decay = does
            for s in order:
                kind, lv = s if isinstance(s, tuple) else (s, 0)
                if decay if kind in ("UTA", "G") else prep if kind in ("K", "LT", "U0", "W0", "N") else rec:
                    yield kind, lv

        def waiter(eng, held=False):
            def wait(q, v):
                if isinstance(v, int):
                    if v > 0:
                        eng.wait_ge(q, START + v)
                elif held:
                    held_wait(eng, q, v, wait_point)
                else:
                    eng.wait_ge(q, START + v)
            return wait

        def cols(tile, h=None):
            return ds(tile * GH, GH) if h is None else ds(tile * GH + h, 1)

        def wide(row):
            return row.unsqueeze(2).to_broadcast([P, GH, P])

        block = ctx.enter_context(nc.Block())

        @block.sync
        def _(sp):
            start_counts(sp, sems[0::5])
            wait = waiter(sp, True)
            sp.dma_start(alog[:], a_log[0:1, :].partition_broadcast(P)).then_inc(rows_loaded, 16)
            sp.dma_start(dtb[:], dt_bias[0:1, :].partition_broadcast(P)).then_inc(rows_loaded, 16)

            def load_kq(tile, par):
                sp.dma_start(kq[par][:], m.qkv_d[ds(tile, 1)].rearrange("t p c i -> p (t c) i")).then_inc(kq_loaded[par], 16)

            def load_gate(tile, par):
                sp.dma_start(gate[:, par].rearrange("p h d -> p (h d)"), m.gate_d[ds(tile * P, P), :]
                             ).then_inc(gate_loaded[par], 16)

            def load_mod(k):
                sp.dma_start(modw[:], w_mod[0, :, 2 * D:].rearrange("(p k) n -> p k n", p=P)[:, ds(k, 1)]
                             .rearrange("p k n -> p (k n)")).then_inc(modw_loaded, 16)

            for n in range(2):
                load_kq(n, n)
                load_gate(n, n)
            load_mod(0)
            sp.wait_ge(rows_zero, 1)
            sp.dma_start(mod_rows[0:1], b_mod[0:1, 2 * D:]).then_inc(bias_loaded, 16)

            def rec(tile, par, more, k=0):
                if more:
                    wait(ks_ready, tile + 1)
                    load_kq(tile + 2, par)
                    if par:
                        wait(mod_scaled, tile * NM + NM)
                        load_mod(k + 1)
                wait(y_ready, tile + 1)
                sp.dma_start(m.y_d[ds(tile * P, P), AH * DV:], y[:].rearrange("p h d -> p (h d)")).then_inc(y_stored, 16)
                if more:
                    load_gate(tile + 2, par)

            with sp.Fori(0, NT // 2 - 1) as i:
                rec(i * 2, 0, True)
                rec(i * 2 + 1, 1, True, i)
            rec(NT - 2, 0, False)
            rec(NT - 1, 1, False)
            sp.wait_ge(y_stored, START + 16 * NT)

        @block.gpsimd
        def _(pool):
            start_counts(pool, sems[1::5])
            wait = waiter(pool, True)
            pool.memset(mod_rows, 0.0).then_inc(rows_zero, 1)
            n = 0
            for lv in range(LV):
                b = 1 << lv
                v = masks[:, lv, :].rearrange("p (n two b) -> p n two b", two=2, b=b)
                pool.memset(masks[:, lv, :], 0.0).then_inc(mask_step, 1)
                n += 1
                pool.wait_ge(mask_step, START + n)
                pool.affine_select(out=v[:, :, 1, :], in_=m.ones[:].rearrange("p (n two b) -> p n two b", two=2, b=b)[:, :, 1, :],
                                   compare_op=ALU.is_ge, fill=0.0, base=0, pattern=[[-2 * b, P // (2 * b)], [0, b]],
                                   channel_multiplier=1).then_inc(mask_step, 1)
                n += 1
                pool.wait_ge(mask_step, START + n)
                pool.affine_select(out=v[:, :, 1, :], in_=v[:, :, 1, :], compare_op=ALU.is_ge, fill=0.0, base=b - 1,
                                   pattern=[[2 * b, P // (2 * b)], [0, b]], channel_multiplier=-1).then_inc(mask_step, 1)
                n += 1
            pool.memset(S[:], 0.0).then_inc(state_zero, 1)
            pool.wait_ge(mask_step, START + n)
            pool.wait_ge(bias_loaded, 16)

            def body(tile, par, does, k):
                nxt = tile + 1
                for kind, lv in parts(does):
                    if kind == "M":
                        wait(mod_scaled, tile * NM + lv + 1)
                        at_ = slice((par * NM + lv) * MW, (par * NM + lv + 1) * MW)
                        pool.tensor_tensor(mod_rows[:, at_], mod_rows[:, at_], mod_part[:], ALU.add).then_inc(mod_added, 1)
                    elif kind == "G":
                        wait(dm_ready, nxt + 2)
                        pool.tensor_scalar(dm[:], dm[:], 0.0, None, ALU.min).then_inc(dm_clamped, 1)
                        wait(exp_ready, nxt + 2)
                        wait(at_ready, nxt + 1)
                        pool.tensor_tensor(em[:], dm[:], m.upper[:].unsqueeze(1).to_broadcast([P, GH, P]), ALU.mult
                                           ).then_inc(em_ready, 1)
                    elif kind == "LT":
                        wait(lt_ready, nxt + 1)
                        wait(xw_ready[1], nxt * NLV)
                        for j in range(LV):
                            pool.tensor_tensor(xt[:, j], lt[:], masks[:, j].unsqueeze(1).to_broadcast([P, GH, P]), ALU.mult
                                               ).then_inc(xt_ready, 1)
                    elif kind == "O1":
                        wait(oss_ready, tile + 1)
                        pool.tensor_scalar(oms[:], oss[:], 1.0 / GD, EPS, ALU.mult, ALU.add).then_inc(o_pow, 1)
                        wait(o_pow, tile * 2 + 1)
                        wait(y_ready, tile)
                        pool.tensor_tensor(orr[:], oms[:], m.half_pow[:, 0:GH], ALU.pow).then_inc(o_pow, 1)

            steps(body, pool)

        @block.scalar
        def _(act):
            start_counts(act, sems[2::5])
            wait = waiter(act)
            act.preload_act_table_set("natural_log_exp_and_others")
            act.wait_ge(pre, START + 4)
            act.activation(absx[:], absx[:], ACT.Exp, scale=-1.0).then_inc(pre, 1)
            act.wait_ge(pre, START + 5)
            act.activation(absx[:], absx[:], ACT.Ln, bias=m.ones[:, 0:1]).then_inc(pre, 1)
            act.activation(alog[:], alog[:], ACT.Exp).then_inc(pre, 1)
            act.activation(bcl[:], bcl[:], ACT.Exp, scale=-1.0).then_inc(pre, 1)
            act.wait_ge(pre, START + 15)
            act.activation(eg[:], gcol[:], ACT.Exp).then_inc(pre, 1)
            act.activation(etot[:], etot[:], ACT.Exp).then_inc(pre, 1)
            act.activation(ekd[:], ekd[:], ACT.Exp).then_inc(pre, 1)
            act.wait_ge(pre, START + 19)

            def body(tile, par, does, k):
                nxt, q = tile + 1, 1 - par
                for kind, lv in parts(does):
                    if kind == "M":
                        wait(modw_loaded, k * 16 + 16)
                        held_wait(act, mod_added, tile * NM + lv, wait_point)
                        act.activation(mod_part[:], modw[:, (par * NM + lv) * MW:(par * NM + lv + 1) * MW], ACT.Copy,
                                       scale=m.c_act[:, ds(k, 1)]).then_inc(mod_scaled, 1)
                    elif kind == "G":
                        wait(dm_clamped, nxt + 2)
                        act.activation(dm[:], dm[:], ACT.Exp).then_inc(exp_ready, 1)
                    elif kind == "VT":
                        wait(vt_ready, tile + 1)
                        wait(r_ready, tile)
                        act.copy(vtok[:], bD[:]).then_inc(v_copied, 1)
                    elif kind == "W0":
                        wait(w0_ready, nxt + 1)
                        for g in range(2):
                            last = act.copy(W[g][:], bB[:, g * H2:(g + 1) * H2])
                        last.then_inc(w0_copied, 1)
                    elif kind == "N":
                        for g in range(2):
                            wait(xw_ready[g], nxt * NLV + lv)
                            act.copy(Y[g][:], bY[g][:]).then_inc(y_copied[g], 1)
                    elif kind == "VN":
                        wait(tr_ready, tile + 1)
                        wait(av_ready, tile)
                        for h in range(GH):
                            last = act.activation(vn[:, h], bA[:, h], ACT.Copy, scale=beta[:, cols(tile, h)])
                        last.then_inc(vn_ready, 1)
                    elif kind == "O1":
                        wait(o_ready, tile + 1)
                        wait(oss_ready, tile)
                        act.activation(osq[:], o[:], ACT.Square).then_inc(osq_ready, 1)

            steps(body, act)

        @block.vector
        def _(dve):
            start_counts(dve, sems[3::5])
            wait = waiter(dve)
            ab3 = m.ab[:].rearrange("p (t e) -> p t e", e=2 * GH)
            dve.wait_ge(rows_loaded, START + 32)
            dve.tensor_scalar(bcl[:], ab3[:, :, GH:], -80.0, None, ALU.max).then_inc(pre, 1)
            dve.tensor_tensor(absx[:], ab3[:, :, 0:GH], dtb[:].unsqueeze(1).to_broadcast([P, NT, GH]), ALU.add).then_inc(pre, 1)
            dve.wait_ge(pre, START + 2)
            dve.tensor_scalar(xs[:], absx[:], 0.0, None, ALU.max).then_inc(pre, 1)
            dve.scalar_tensor_tensor(out=absx[:], in0=absx[:], scalar=-1.0, in1=absx[:], op0=ALU.mult, op1=ALU.max).then_inc(pre, 1)
            dve.wait_ge(pre, START + 8)
            dve.tensor_tensor(sp_[:], xs[:], absx[:], ALU.add).then_inc(pre, 1)
            dve.wait_ge(pre, START + 9)
            al3 = alpha[:].rearrange("p (t h) -> p t h", h=GH)
            dve.scalar_tensor_tensor(out=al3, in0=sp_[:], scalar=-1.0, in1=alog[:].unsqueeze(1).to_broadcast([P, NT, GH]),
                                     op0=ALU.mult, op1=ALU.mult).then_inc(pre, 1)
            dve.tensor_scalar(bcl[:], bcl[:], 1.0, None, ALU.add).then_inc(pre, 1)
            dve.wait_ge(pre, START + 11)
            dve.reciprocal(beta[:].rearrange("p (t h) -> p t h", h=GH), bcl[:]).then_inc(pre, 1)
            dve.wait_ge(grow_ready, START + 1)
            dve.tensor_copy(gcol[:], bA[:, 0, 0:NT * GH]).then_inc(pre, 1)
            dve.tensor_copy(etot[:], bB[:, 0, 0:NT * GH]).then_inc(pre, 1)
            dve.wait_ge(pre, START + 14)
            dve.tensor_tensor(ekd[:], etot[:], gcol[:], ALU.subtract).then_inc(pre, 1)
            dve.wait_ge(pre, START + 18)
            dve.tensor_scalar(neg_eg[:], eg[:], -1.0, None, ALU.mult).then_inc(pre, 1)
            dve.wait_ge(pre, START + 19)

            def body(tile, par, does, k):
                nxt, q = tile + 1, 1 - par
                for kind, lv in parts(does):
                    if kind == "UTA":
                        wait(grow_ready, nxt + 2)
                        dve.tensor_tensor(uta[:], m.upper[:].unsqueeze(1).to_broadcast([P, GH, P]), wide(alpha[:, cols(tile + 2)]),
                                          ALU.mult).then_inc(uta_ready, 1)
                    elif kind == "G":
                        wait(grow_ready, nxt + 3)
                        wait(em_ready, nxt + 1)
                        dve.tensor_tensor(dm[:], bA[:], wide(gcol[:, cols(tile + 2)]), ALU.subtract).then_inc(dm_ready, 1)
                    elif kind == "KD":
                        wait(kt_ready, tile + 1)
                        wait(ds_ready, tile)
                        dve.tensor_tensor(kd[:], bA[:], wide(ekd[:, cols(tile)]), ALU.mult).then_inc(kd_ready, 1)
                    elif kind == "LT":
                        wait(kk_ready, nxt + 1)
                        wait(em_ready, nxt + 1)
                        wait(xt_ready, nxt * LV)
                        for h in range(GH):
                            b = (bB, bC)[h // 2]
                            last = dve.scalar_tensor_tensor(out=lt[:, h], in0=b[:, (h % 2) * 2], scalar=beta[:, cols(nxt, h)],
                                                            in1=em[:, h], op0=ALU.mult, op1=ALU.mult)
                        last.then_inc(lt_ready, 1)
                        wait(av_ready, tile)
                        for g in range(2):
                            last = dve.tensor_tensor(at[q][:, g * 2:g * 2 + 2],
                                                     (bB, bC)[g][:].rearrange("p (h two) i -> p h two i", two=2)[:, :, 1],
                                                     em[:, g * 2:g * 2 + 2], ALU.mult)
                        last.then_inc(at_ready, 1)
                    elif kind == "U0":
                        wait(xt_ready, nxt * LV + 1)
                        wait(tr_ready, tile)
                        dve.tensor_tensor(U[q][:], m.ident[:].unsqueeze(1).to_broadcast([P, GH, P]), xt[:, 0], ALU.subtract
                                          ).then_inc(u0_ready, 1)
                    elif kind == "KS":
                        wait(ks_ready, tile + 1)
                        wait(v_copied, tile + 1)
                        for h in range(GH):
                            last = dve.scalar_tensor_tensor(out=R[:, h], in0=bC[:, h], scalar=neg_eg[:, cols(tile, h)],
                                                            in1=vtok[:, h], op0=ALU.mult, op1=ALU.add)
                        last.then_inc(r_ready, 1)
                        dve.tensor_tensor(qs[:], bD[:], wide(eg[:, cols(tile)]), ALU.mult).then_inc(qs_ready, 1)
                    elif kind == "N":
                        for g in range(2):
                            wait(wy_ready[g], nxt * NLV + lv)
                            if lv < NLV:
                                dve.tensor_tensor(W[g][:], W[g][:], bW[g][:, 0], ALU.subtract)
                            ug = U[q][:, g * H2:(g + 1) * H2]
                            dve.tensor_tensor(ug, ug, bW[g][:, 1], ALU.subtract).then_inc(uw_updated[g], 1)
                    elif kind == "AV":
                        wait(ds_ready, tile + 1)
                        for h in range(GH):
                            last = dve.scalar_tensor_tensor(out=S[:, h], in0=S[:, h], scalar=etot[:, cols(tile, h)],
                                                            in1=bC[:, h], op0=ALU.mult, op1=ALU.add)
                        last.then_inc(state_ready, 1)
                        wait(av_ready, tile + 1)
                        wait(qs_ready, tile + 1)
                        wait(y_ready, tile)
                        dve.tensor_tensor(o[:], qs[:], bB[:], ALU.add).then_inc(o_ready, 1)
                    elif kind == "O1":
                        wait(osq_ready, tile + 1)
                        wait(o_pow, tile * 2)
                        dve.tensor_reduce(oss[:], osq[:], AX.X, ALU.add).then_inc(oss_ready, 1)
                    elif kind == "O2":
                        wait(o_pow, tile * 2 + 2)
                        wait(y_stored, tile * 16)
                        wait(gate_loaded[par], (tile - par) * 8 + 16)
                        for h in range(GH):
                            last = dve.scalar_tensor_tensor(out=y[:, h], in0=o[:, h], scalar=orr[:, h:h + 1],
                                                            in1=gate[:, par, h], op0=ALU.mult, op1=ALU.mult)
                        last.then_inc(y_ready, 1)

            steps(body, dve)

        @block.tensor
        def _(pe):
            start_counts(pe, sems[4::5])
            wait = waiter(pe)
            pe.wait_ge(pre, START + 12)
            pe.matmul(bA[:, 0, 0:NT * GH], m.upper[:], alpha[:], start=True, stop=True)
            pe.matmul(bB[:, 0, 0:NT * GH], m.ones[:], alpha[:], start=True, stop=True).then_inc(grow_ready, 1)
            pe.wait_ge(pre, START + 14)
            pe.wait_ge(state_zero, START + 1)

            def body(tile, par, does, k):
                nxt, q = tile + 1, 1 - par
                for kind, lv in parts(does):
                    if kind == "G":
                        wait(uta_ready, nxt + 2)
                        wait(vn_ready, nxt)
                        pe.matmul(bA[:].rearrange("p h i -> p (h i)"), m.ones[:], uta[:].rearrange("p h i -> p (h i)"),
                                  start=True, stop=True).then_inc(grow_ready, 1)
                    elif kind == "K":
                        wait(kq_loaded[q], (nxt - q) * 8 + 16)
                        wait(o_ready, tile)
                        wait(state_ready, tile)
                        for h in range(GH):
                            out = (bB, bC)[h // 2][:, (h % 2) * 2:(h % 2) * 2 + 2].rearrange("p a i -> p (a i)")
                            last = pe.matmul(out, kq[q][:, 2 * h, :], kq[q][:, 2 * h:2 * h + 2, :].rearrange("p a i -> p (a i)"),
                                             start=True, stop=True)
                        last.then_inc(kk_ready, 1)
                    elif kind == "VT":
                        wait(qs_ready, tile)
                        for h in range(GH):
                            last = pe.transpose(bD[:, h], kq[par][:, 2 * GH + h, :], m.ident[:])
                        last.then_inc(vt_ready, 1)
                    elif kind == "KD":
                        if does[0]:
                            wait(dm_ready, nxt + 1)
                        else:
                            wait(vn_ready, tile)
                        for h in range(GH):
                            last = pe.transpose(bA[:, h], kq[par][:, 2 * h, :], m.ident[:])
                        last.then_inc(kt_ready, 1)
                    elif kind == "W0":
                        wait(u0_ready, nxt + 1)
                        wait(at_ready, nxt + 1)
                        for h in range(GH):
                            last = pe.transpose(bB[:, h], U[q][:, h], m.ident[:])
                        last.then_inc(w0_ready, 1)
                    elif kind == "KS":
                        if does[0]:
                            wait(at_ready, nxt + 1)
                        wait(state_ready, tile)
                        wait(v_copied, tile + 1)
                        for h in range(GH):
                            pe.matmul(bC[:, h], kq[par][:, 2 * h, :], S[:, h], start=True, stop=True)
                        for h in range(GH):
                            last = pe.matmul(bD[:, h], kq[par][:, 2 * h + 1, :], S[:, h], start=True, stop=True)
                        last.then_inc(ks_ready, 1)
                    elif kind == "N":
                        wait(xt_ready, nxt * LV + 1 + lv)
                        for g in range(2):
                            if lv == 1:
                                wait(w0_copied, nxt + 1)
                            else:
                                wait(uw_updated[g], nxt * NLV + lv - 1)
                            for h in range(H2):
                                last = pe.matmul(bY[g][:, h], xt[:, lv, g * H2 + h], W[g][:, h], start=True, stop=True)
                            last.then_inc(xw_ready[g], 1)
                        for g in range(2):
                            wait(y_copied[g], nxt * NLV + lv)
                            for h in range(H2):
                                if lv < NLV:
                                    pe.matmul(bW[g][:, 0, h], U[q][:, g * H2 + h], Y[g][:, h], start=True, stop=True)
                                last = pe.matmul(bW[g][:, 1, h], Y[g][:, h], U[q][:, g * H2 + h], start=True, stop=True)
                            last.then_inc(wy_ready[g], 1)
                    elif kind == "TR":
                        wait(r_ready, tile + 1)
                        wait(kd_ready, tile + 1)
                        for g in range(2):
                            wait(uw_updated[g], tile * NLV + NLV)
                        for h in range(GH):
                            last = pe.matmul(bA[:, h], U[par][:, h], R[:, h], start=True, stop=True)
                        last.then_inc(tr_ready, 1)
                    elif kind == "AV":
                        wait(vn_ready, tile + 1)
                        wait(o_ready, tile)
                        if does[0]:
                            wait(w0_copied, nxt + 1)
                        for h in range(GH):
                            last = pe.matmul(bC[:, h], kd[:, h], vn[:, h], start=True, stop=True)
                        last.then_inc(ds_ready, 1)
                        for h in range(GH):
                            last = pe.matmul(bB[:, h], at[par][:, h], vn[:, h], start=True, stop=True)
                        last.then_inc(av_ready, 1)

            steps(body, pe)


def attention(nc, m):
    SCALE = QK ** -0.5
    units = [(i, h) for i in range(NT) for h in range(AH)]
    nblk = [i // 4 + 1 for i, _ in units]
    base = [sum(nblk[:u]) for u in range(len(units) + 1)]
    NU = len(units)
    RING = 8
    blocks = [(u, b) for u in range(NU) for b in range(nblk[u])]
    ahead = [max(w for w in range(NU) if base[w + 1] <= base[u + 1] + 4) for u in range(NU)]
    nmax = [nblk[u] + (1 if units[u][0] % 4 else 0) for u in range(NU)]
    max0 = [sum(nmax[:u]) for u in range(NU + 1)]

    KV = [0, 1, 2, 4, 8, 12, NT]

    def width(i, b):
        return min(4, i + 1 - 4 * b)

    with nc.cleanup_on_exit(), ExitStack() as ctx:
        sb = lambda n, s, d=F32: ctx.enter_context(nc.sbuf_tensor(n, s, d))
        ps = lambda n, s: ctx.enter_context(nc.psum_tensor(n, s, F32))
        sem = nc.alloc_semaphore
        kT, v = sb("keys", [QK, NT, AH, P]), sb("values", [P, NT, AH * DV])
        qT = sb("queries", [QK, 2, AH, P])
        mask = sb("diag_mask", [P, P])
        mx, top, nbias = sb("block_max", [P, 5]), sb("row_max", [P, 1]), sb("neg_max", [P, RING])
        prob, probT = sb("probs", [P, RING, 4, P]), sb("probs_T", [P, RING, 4, P])
        sums, den, rden = sb("exp_sums", [P, 2, AH, 4]), sb("denominator", [P, AH]), sb("inv_denominator", [P, AH])
        o, y, junk = sb("attn_out", [P, AH, DV]), sb("attn_y", [P, AH * DV]), sb("attn_junk", [P, AH * DV])
        oss, oms, orr = sb("attn_sumsq", [P, 1]), sb("attn_meansq", [P, 1]), sb("attn_rstd", [P, 1])
        zeros = sb("zero_rows", [P, D])
        pS = ps("scores", [P, 4, 512])
        pT = [ps(f"probsT_ps{i}", [P, 4, P]) for i in range(2)]
        pO = [ps(f"attn_ps{i}", [P, AH, DV]) for i in range(2)]
        kv_loaded = [sem(f"kv_loaded{s}") for s in range(len(KV) - 1)]
        q_loaded = [sem(f"q_loaded{i}") for i in range(2)]
        mask_made, zeros_stored = sem("mask_made"), sem("zeros_stored")
        s_ready, max_step, top_ready, nbias_ready, exp_done = (sem(n) for n in (
            "s_ready", "max_step", "top_ready", "nbias_ready", "exp_done"))
        t_ready, pv_ready = sem("t_ready"), sem("pv_ready")
        t_copied = [sem("t_copied_dve"), sem("t_copied_act")]
        den_step, o_squared, o_pow, y_ready, y_stored = (sem(n) for n in (
            "den_step", "o_squared", "o_pow3", "y_ready3", "y_stored3"))

        def waiter(eng):
            def wait(q, value):
                if value > 0:
                    eng.wait_ge(q, value)
            return wait

        block = ctx.enter_context(nc.Block())

        def load_kv(eng, n):
            t, end = KV[n], KV[n + 1]
            if n < 2:
                eng.dma_start(qT[:, n].rearrange("p h t -> p (h t)"), m.qT_d[n * QK:(n + 1) * QK, :]).then_inc(q_loaded[n], 16)
            eng.dma_start(kT[:, t:end].rearrange("p t h k -> p t (h k)"),
                          m.kT_d[t * QK:end * QK, :].rearrange("(t p) n -> p t n", p=QK)).then_inc(kv_loaded[n], 16)
            eng.dma_start(v[:, t:end], m.v_d[t * P:end * P, :].rearrange("(t p) n -> p t n", p=P)).then_inc(kv_loaded[n], 16)

        @block.sync
        def _(sp):
            wait = waiter(sp)
            load_kv(sp, 2)
            nsure = 2 * T // P
            per = (NB - nsure) // NT
            assert per * NT == NB - nsure
            sp.wait_ge(mask_made, 3)
            for i in range(NT):
                if i + 2 < NT:
                    wait(s_ready, base[AH * (i + 1)])
                    sp.dma_start(qT[:, i % 2].rearrange("p h t -> p (h t)"), m.qT_d[(i + 2) * QK:(i + 3) * QK, :]
                                 ).then_inc(q_loaded[i % 2], 16)
                for n in range(3, len(KV) - 1):
                    if i == max(0, KV[n] - 5):
                        load_kv(sp, n)
                sp.dma_start(m.ys_d[(nsure + i * per) * P:(nsure + (i + 1) * per) * P, :].rearrange("(b p) n -> p b n", p=P),
                             zeros[:].unsqueeze(1).to_broadcast([P, per, D])).then_inc(zeros_stored, 16)
                if i >= 1:
                    wait(y_ready, i)
                    sp.dma_start(m.y_d[(i - 1) * P:i * P, 0:AH * DV], y[:]).then_inc(y_stored, 16)
            wait(y_ready, NT)
            sp.dma_start(m.y_d[(NT - 1) * P:, 0:AH * DV], y[:]).then_inc(y_stored, 16)
            sp.wait_ge(y_stored, 16 * NT)
            sp.wait_ge(zeros_stored, 16 * NT)

        @block.gpsimd
        def _(pool):
            pool.memset(zeros[:], 0.0).then_inc(mask_made, 1)
            pool.memset(mask[:], 0.0).then_inc(mask_made, 1)
            pool.wait_ge(mask_made, 2)
            pool.affine_select(out=mask[:], in_=mask[:], compare_op=ALU.is_ge, fill=NEG, base=0,
                               pattern=[[-1, P]], channel_multiplier=1).then_inc(mask_made, 1)
            for i in range(NT):
                pool.wait_ge(o_squared, i + 1)
                pool.tensor_scalar(oms[:], oss[:], 1.0 / (AH * DV), EPS, ALU.mult, ALU.add).then_inc(o_pow, 1)
                pool.wait_ge(o_pow, 2 * i + 1)
                if i:
                    pool.wait_ge(y_ready, i)
                pool.tensor_tensor(orr[:], oms[:], m.half_pow[:, 0:1], ALU.pow).then_inc(o_pow, 1)

        def tail_of(u):
            i, h = units[u]
            return i - 1 if h == 2 and i >= 1 else (NT - 1 if u == NU - 1 else None)

        @block.scalar
        def _(act):
            wait = waiter(act)
            load_kv(act, 0)
            load_kv(act, 1)

            def exp(u, b):
                i, h = units[u]
                s = base[u] + b
                wait(nbias_ready, u + 1)
                wait(t_ready, s - RING + 1)
                if i >= 2 and h == 0 and b == 0:
                    wait(den_step, 3 * (i - 1))
                n = width(i, b) * P
                act.activation(prob[:, s % RING, 0:n // P].rearrange("p t k -> p (t k)"), pS[:, s % 4, 0:n], ACT.Exp,
                               scale=SCALE, bias=nbias[:, u % RING:u % RING + 1], accum_out=sums[:, i % 2, h, b:b + 1]
                               ).then_inc(exp_done, 1)

            def copy_out(u, g):
                s = base[u] + g
                wait(t_ready, s + 1)
                wait(pv_ready, s - RING + 1)
                n = width(units[u][0], g)
                act.copy(probT[:, s % RING, 0:n], pT[1][:, 0:n]).then_inc(t_copied[1], 1)

            for s in range(base[ahead[0]]):
                exp(*blocks[s])
            done = base[ahead[0]]
            for u in range(NU):
                later = blocks[done:base[ahead[u] + 1]]
                done = base[ahead[u] + 1]
                for g in range(nblk[u]):
                    if (base[u] + g) % 2 == 1:
                        copy_out(u, g)
                        if later:
                            exp(*later.pop(0))
                for s in later:
                    exp(*s)
                if (i := tail_of(u)) is not None:
                    wait(den_step, 3 * i + 3)
                    act.activation(junk[:], o[:].rearrange("p h d -> p (h d)"), ACT.Square, accum_out=oss[:]).then_inc(o_squared, 1)
                    wait(o_pow, 2 * i + 2)
                    wait(y_stored, 16 * i)
                    act.activation(y[:], o[:].rearrange("p h d -> p (h d)"), ACT.Copy, scale=orr[:, 0:1]).then_inc(y_ready, 1)

        @block.vector
        def _(dve):
            wait = waiter(dve)
            dve.wait_ge(mask_made, 3)

            def maxima(u):
                i, h = units[u]
                n = max0[u]
                wait(nbias_ready, u)
                for b in range(nblk[u]):
                    wait(s_ready, base[u] + b + 1)
                    w = width(i, b) * P
                    if b == nblk[u] - 1:
                        w -= P
                        dve.tensor_tensor_reduce(pS[:, (base[u] + b) % 4, w:w + P], pS[:, (base[u] + b) % 4, w:w + P], mask[:], 1.0, NEG, ALU.add, ALU.max,
                                                 mx[:, nblk[u]:nblk[u] + 1] if w else mx[:, b:b + 1]).then_inc(max_step, 1)
                        n += 1
                    if w:
                        dve.tensor_reduce(mx[:, b:b + 1], pS[:, (base[u] + b) % 4, 0:w], AX.X, ALU.max).then_inc(max_step, 1)
                        n += 1
                assert n == max0[u + 1]
                wait(max_step, n)
                best = mx
                if nmax[u] > 1:
                    dve.tensor_reduce(top[:], mx[:, 0:nmax[u]], AX.X, ALU.max).then_inc(top_ready, 1)
                    wait(top_ready, sum(k > 1 for k in nmax[:u + 1]))
                    best = top
                if u >= RING:
                    wait(exp_done, base[u - RING + 1])
                dve.tensor_scalar(nbias[:, u % RING:u % RING + 1], best[:, 0:1], -SCALE, None, ALU.mult).then_inc(nbias_ready, 1)

            for w in range(ahead[0]):
                maxima(w)
            seen = ahead[0]
            for u in range(NU):
                for w in range(seen, ahead[u] + 1):
                    maxima(w)
                seen = ahead[u] + 1
                for g in range(nblk[u]):
                    if (base[u] + g) % 2 == 0:
                        s = base[u] + g
                        wait(t_ready, s + 1)
                        wait(pv_ready, s - RING + 1)
                        n = width(units[u][0], g)
                        dve.tensor_copy(probT[:, s % RING, 0:n], pT[0][:, 0:n]).then_inc(t_copied[0], 1)
                if (i := tail_of(u)) is not None:
                    nb = i // 4 + 1
                    wait(exp_done, base[AH * (i + 1)])
                    dve.tensor_reduce(den[:], sums[:, i % 2, :, 0:nb], AX.X, ALU.add).then_inc(den_step, 1)
                    wait(den_step, 3 * i + 1)
                    dve.reciprocal(rden[:], den[:]).then_inc(den_step, 1)
                    wait(den_step, 3 * i + 2)
                    wait(pv_ready, base[AH * (i + 1)])
                    wait(y_ready, i)
                    dve.tensor_tensor(o[:], pO[i % 2][:], rden[:].unsqueeze(2).to_broadcast([P, AH, DV]), ALU.mult
                                      ).then_inc(den_step, 1)

        @block.tensor
        def _(pe):
            wait = waiter(pe)

            def scores(u):
                i, h = units[u]
                if h == 0:
                    wait(q_loaded[i % 2], 16 * (i // 2 + 1))
                    if i in KV:
                        wait(kv_loaded[KV.index(i)], 32)
                for b in range(nblk[u]):
                    wait(exp_done, base[u] + b - 3)
                    n = width(i, b)
                    pe.matmul(pS[:, (base[u] + b) % 4, 0:n * P], qT[:, i % 2, h], kT[:, 4 * b:4 * b + n, h, :], start=True, stop=True
                              ).then_inc(s_ready, 1)

            def values(u, g):
                i, h = units[u]
                gi = base[u] + g
                wait(t_copied[gi % 2], gi // 2 + 1)
                if g == 0 and h == 0 and i >= 2:
                    wait(den_step, 3 * (i - 1))
                for t in range(width(i, g)):
                    kt = 4 * g + t
                    last = pe.matmul(pO[i % 2][:, h], probT[:, gi % RING, t], v[:, kt, h * DV:(h + 1) * DV],
                                     start=(kt == 0), stop=(kt == i))
                last.then_inc(pv_ready, 1)

            for w in range(ahead[0]):
                scores(w)
            asked = ahead[0]
            for u in range(NU):
                i, h = units[u]
                for w in range(asked, ahead[u] + 1):
                    scores(w)
                asked = ahead[u] + 1
                for g in range(nblk[u]):
                    gi = base[u] + g
                    wait(exp_done, gi + 1)
                    wait(t_copied[gi % 2], gi // 2)
                    n = width(i, g)
                    for t in range(n):
                        last = pe.transpose(pT[gi % 2][:, t], prob[:, gi % RING, t], m.ident[:])
                    last.then_inc(t_ready, 1)
                    if gi:
                        values(*blocks[gi - 1])
            values(*blocks[-1])


def output(nc, m, x, mla_out_norm, gdn_out_norm, w_out, w_route_group, b_route_group, w_route_expert, b_route_expert,
           moe_norm, w1, w3, w2):
    NR = NG + NE
    with nc.cleanup_on_exit(), ExitStack() as ctx:
        sb = lambda n, s, d=F32: ctx.enter_context(nc.sbuf_tensor(n, s, d))
        ps = lambda n, s: ctx.enter_context(nc.psum_tensor(n, s, F32))
        sems = []

        def sem(name):
            sems.append(nc.alloc_semaphore(name))
            return sems[-1]

        nrow = sb("norm_row", [P, D])
        wo, wr = sb("w_out_sb", [P, ND, D]), sb("w_route", [P, ND, NR])
        ogain, rbias = sb("out_gain", [P, 5]), sb("route_bias", [P, NR])
        yin, xres = sb("y_in", [P, 2, D]), sb("x_res", [P, 2, D])
        yT = [sb(f"yT{i}", [P, ND, P]) for i in range(2)]
        upd, x1 = sb("x_update", [P, D]), sb("x1_tile", [P, D])
        h2, h2T = sb("h2_tile", [P, D]), sb("h2T", [P, ND, P])
        junk = sb("junk4", [P, D])
        ss, ms, rs = sb("x1_sumsq", [P, 1]), sb("x1_meansq", [P, 1]), sb("x1_rstd", [P, 1])
        pT, pX, pH = ps("yT_ps", [P, 2, 512]), ps("out_ps", [P, 2, 512]), ps("h2T_ps", [P, 2, 512])
        pL = ps("logits_ps", [P, NR])
        norm_loaded, mod_summed, mod_made = (nc.alloc_semaphore(n) for n in ("norm_loaded", "mod_summed", "mod_made"))
        w_loaded, w_scaled, wait_point = sem("w_loaded4"), sem("w_scaled4"), sem("wait_point4")
        y_loaded, x_loaded = [sem(f"y_loaded{i}") for i in range(2)], [sem(f"xr_loaded{i}") for i in range(2)]
        yT_ready, yT_act, yT_dve, out_ready = sem("yT_ready"), sem("yT_act"), sem("yT_dve"), sem("out_ready")
        upd_ready, x1_ready, x1_squared, x1_pow = sem("upd_ready"), sem("x1_ready"), sem("x1_squared"), sem("x1_pow")
        h2_scaled, h2_ready, x1_stored, h2_stored = sem("h2_scaled"), sem("h2_ready"), sem("x1_stored"), sem("h2_stored")
        h2T_ready, h2T_act, h2T_dve, logit_ready, logit_read = (
            sem("h2T_ready"), sem("h2T_act"), sem("h2T_dve"), sem("logit_ready"), sem("logit_read"))
        sems += m.expert_loaded

        def steps(body, eng):
            body(-1, 1, True, False, False)
            body(0, 0, True, True, False)
            with eng.Fori(0, NT // 2 - 1) as i:
                body(i * 2 + 1, 1, True, True, True)
                body(i * 2 + 2, 0, True, True, True)
            body(NT - 1, 1, False, True, True)
            body(NT, 0, False, False, True)

        def waiter(eng, held=False):
            def wait(q, v):
                if isinstance(v, int):
                    if v > 0:
                        eng.wait_ge(q, START + v)
                elif held:
                    held_wait(eng, q, v, wait_point)
                else:
                    eng.wait_ge(q, START + v)
            return wait

        block = ctx.enter_context(nc.Block())

        @block.sync
        def _(sp):
            start_counts(sp, sems[0::5])
            wait = waiter(sp, True)
            sp.dma_start(nrow[:], moe_norm[0:1, :].partition_broadcast(P)).then_inc(norm_loaded, 16)
            sp.dma_start(ogain[:, 0:4], mla_out_norm[0].rearrange("(k p) -> p k", p=P)).then_inc(w_loaded, 16)
            sp.dma_start(ogain[:, 4:5], gdn_out_norm[0].rearrange("(k p) -> p k", p=P)).then_inc(w_loaded, 16)
            sp.dma_start(wo[:], w_out[0].rearrange("(k p) n -> p k n", p=P)).then_inc(w_loaded, 16)
            sp.dma_start(wr[:, :, 0:NG], w_route_group[0].rearrange("(k p) n -> p k n", p=P)).then_inc(w_loaded, 16)
            sp.dma_start(wr[:, :, NG:], w_route_expert[0].rearrange("(k p) n -> p k n", p=P)).then_inc(w_loaded, 16)
            sp.dma_start(rbias[:, 0:NG], b_route_group[0:1, :].partition_broadcast(P)).then_inc(w_loaded, 16)
            sp.dma_start(rbias[:, NG:], b_route_expert[0:1, :].partition_broadcast(P)).then_inc(w_loaded, 16)

            def load(tile, par):
                sp.dma_start(yin[:, par], m.y_d[ds(tile * P, P), :]).then_inc(y_loaded[par], 16)
                sp.dma_start(xres[:, par], x[0, ds(tile * P, P), :]).then_inc(x_loaded[par], 16)

            def store(tile):
                wait(x1_ready, tile + 1)
                sp.dma_start(m.x1_d[ds(tile * P, P), :], x1[:]).then_inc(x1_stored, 16)
                wait(h2_ready, tile + 1)
                sp.dma_start(m.h2_d[ds(tile * P, P), :], h2[:]).then_inc(h2_stored, 16)

            load(0, 0)
            load(1, 1)
            for e in range(WSLOTS):
                load_expert(sp, m, w1, w3, w2, e, e)
            with sp.Fori(0, NT // 2 - 1) as i:
                for par in range(2):
                    store(i * 2 + par)
                    load(i * 2 + par + 2, par)
            store(NT - 2)
            store(NT - 1)
            sp.wait_ge(x1_stored, START + 16 * NT)
            sp.wait_ge(h2_stored, START + 16 * NT)

        @block.gpsimd
        def _(pool):
            start_counts(pool, sems[1::5])
            wait = waiter(pool, True)
            pool.wait_ge(mod_made, 4)

            def body(n, par, ty, mm, rt):
                if mm:
                    wait(upd_ready, n + 1)
                    wait(x_loaded[par], (n - par) * 8 + 16)
                    wait(h2_scaled, n)
                    wait(x1_stored, n * 16)
                    pool.tensor_tensor(x1[:], upd[:], xres[:, par], ALU.add).then_inc(x1_ready, 1)
                    wait(x1_squared, n + 1)
                    pool.tensor_scalar(ms[:], ss[:], 1.0 / D, EPS, ALU.mult, ALU.add).then_inc(x1_pow, 1)
                    wait(x1_pow, n * 2 + 1)
                    pool.tensor_tensor(rs[:], ms[:], m.half_pow[:, 0:1], ALU.pow).then_inc(x1_pow, 1)
                    wait(h2_scaled, n + 1)
                    pool.tensor_tensor(h2[:], h2[:], m.shift_m, ALU.add).then_inc(h2_ready, 1)

            steps(body, pool)

        @block.scalar
        def _(act):
            start_counts(act, sems[2::5])
            wait = waiter(act)
            act.wait_ge(w_loaded, START + 16 * 7)
            for k in range(ND):
                last = act.activation(wo[:, k], wo[:, k], ACT.Copy, scale=ogain[:, min(k, 4):min(k, 4) + 1])
            last.then_inc(w_scaled, 1)

            def body(n, par, ty, mm, rt):
                if rt:
                    wait(h2T_ready, n)
                    wait(logit_ready, n - 1)
                    act.copy(h2T[:, 0:4].rearrange("p k t -> p (k t)"), pH[:, 0]).then_inc(h2T_act, 1)
                if ty:
                    wait(yT_ready, n + 2)
                    act.copy(yT[1 - par][:, 0:4].rearrange("p k t -> p (k t)"), pT[:, 0]).then_inc(yT_act, 1)
                if mm:
                    wait(x1_ready, n + 1)
                    act.activation(junk[:], x1[:], ACT.Square, accum_out=ss[:]).then_inc(x1_squared, 1)

            steps(body, act)

        @block.vector
        def _(dve):
            start_counts(dve, sems[3::5])
            wait = waiter(dve)
            for part in range(4):
                row, total = m.mod_rows[:, part], (pX, pH, pT, pX)[part][:].rearrange("p b n -> p (b n)")
                dve.wait_ge(mod_summed, part + 1)
                if part == 2:
                    dve.wait_ge(norm_loaded, 16)
                    dve.scalar_tensor_tensor(out=row, in0=total, scalar=1.0, in1=nrow[:], op0=ALU.add, op1=ALU.mult
                                             ).then_inc(mod_made, 1)
                else:
                    dve.tensor_copy(row, total).then_inc(mod_made, 1)
            dve.wait_ge(mod_made, 4)
            dve.wait_ge(w_loaded, START + 16 * 7)

            def body(n, par, ty, mm, rt):
                if mm:
                    wait(out_ready, n + 1)
                    wait(x1_ready, n)
                    dve.tensor_tensor(upd[:], pX[:].rearrange("p b n -> p (b n)"), m.gate_a, ALU.mult).then_inc(upd_ready, 1)
                if rt:
                    wait(h2T_ready, n)
                    wait(logit_ready, n - 1)
                    dve.tensor_copy(h2T[:, 4:8].rearrange("p k t -> p (k t)"), pH[:, 1]).then_inc(h2T_dve, 1)
                if ty:
                    wait(yT_ready, n + 2)
                    dve.tensor_copy(yT[1 - par][:, 4:8].rearrange("p k t -> p (k t)"), pT[:, 1]).then_inc(yT_dve, 1)
                if rt:
                    wait(logit_ready, n)
                    dve.tensor_tensor(m.logits[:, ds((n - 1) * NR, NR)], pL[:], rbias[:], ALU.add).then_inc(logit_read, 1)
                if mm:
                    wait(x1_pow, n * 2 + 2)
                    wait(h2T_ready, n)
                    wait(h2_stored, n * 16)
                    dve.scalar_tensor_tensor(out=h2[:], in0=x1[:], scalar=rs[:, 0:1], in1=m.gain_m, op0=ALU.mult,
                                             op1=ALU.mult).then_inc(h2_scaled, 1)

            steps(body, dve)

        @block.tensor
        def _(pe):
            start_counts(pe, sems[4::5])
            wait = waiter(pe)
            for part in range(4):
                if part == 3:
                    pe.wait_ge(mod_made, 1)
                for half in range(2):
                    last = pe.matmul((pX, pH, pT, pX)[part][:, half], m.ones[:], m.mod_rows[:, part, half * 512:(half + 1) * 512],
                                     start=True, stop=True)
                last.then_inc(mod_summed, 1)
            pe.wait_ge(mod_made, 4)
            pe.wait_ge(w_loaded, START + 16 * 7)
            pe.wait_ge(w_scaled, START + 1)

            def body(n, par, ty, mm, rt):
                if mm:
                    wait(yT_act, n + 1)
                    wait(yT_dve, n + 1)
                    wait(upd_ready, n)
                    for half in range(2):
                        for k in range(ND):
                            last = pe.matmul(pX[:, half], yT[par][:, k], wo[:, k, half * 512:(half + 1) * 512],
                                             start=(k == 0), stop=(k == ND - 1))
                    last.then_inc(out_ready, 1)
                if rt:
                    wait(h2_ready, n)
                    wait(h2T_act, n - 1)
                    wait(h2T_dve, n - 1)
                    for k in range(ND):
                        last = pe.transpose(pH[:, k // 4, (k % 4) * P:(k % 4 + 1) * P], h2[:, k * P:(k + 1) * P], m.ident[:])
                    last.then_inc(h2T_ready, 1)
                if ty:
                    q = 1 - par
                    wait(y_loaded[q], (n + 1 - q) * 8 + 16)
                    wait(yT_act, n + 1)
                    wait(yT_dve, n + 1)
                    for k in range(ND):
                        last = pe.transpose(pT[:, k // 4, (k % 4) * P:(k % 4 + 1) * P], yin[:, q, k * P:(k + 1) * P], m.ident[:])
                    last.then_inc(yT_ready, 1)
                if rt:
                    wait(h2T_act, n)
                    wait(h2T_dve, n)
                    wait(logit_read, n - 1)
                    for k in range(ND):
                        last = pe.matmul(pL[:], h2T[:, k], wr[:, k], start=(k == 0), stop=(k == ND - 1))
                    last.then_inc(logit_ready, 1)

            steps(body, pe)


WSLOTS = 4


def load_expert(sp, m, w1, w3, w2, e, slot):
    sp.dma_start(m.w13[:, slot, :, 0:DE], w1[0, ds(e, 1)].rearrange("e (k p) n -> p (e k) n", p=P)).then_inc(m.expert_loaded[slot], 16)
    sp.dma_start(m.w13[:, slot, :, DE:], w3[0, ds(e, 1)].rearrange("e (k p) n -> p (e k) n", p=P)).then_inc(m.expert_loaded[slot], 16)
    sp.dma_start(m.w2b[:, slot], w2[0, ds(e, 1)].rearrange("e (k p) n -> p (e k) n", p=P)).then_inc(m.expert_loaded[slot], 16)


NB = -(-2 * T // P) + NE
NBT = NB + 2


def routing(nc, m):
    NR = NG + NE
    with nc.cleanup_on_exit(), ExitStack() as ctx:
        sb = lambda n, s, d=F32: ctx.enter_context(nc.sbuf_tensor(n, s, d))
        ps = lambda n, s: ctx.enter_context(nc.psum_tensor(n, s, F32))
        sem = nc.alloc_semaphore
        gmax, gsum, pg = sb("group_max", [P, NT]), sb("group_sum", [P, NT]), sb("group_prob", [P, NT])
        gx, gh = sb("group_exp", [P, NT, NG]), sb("group_hot", [P, NT, NG])
        prod = sb("group_le", [P, NT, NG, EG])
        le, hot = sb("le", [P, NT, EG]), [sb(f"hot{k}", [P, NT, EG]) for k in range(2)]
        tmp = sb("first_tmp", [P, NT, EG])
        top = [sb(f"top{k}", [P, NT]) for k in range(2)]
        first = sb("first_max", [P, NT])
        e21, den = sb("exp_gap", [P, NT]), sb("gate_den", [P, NT])
        E = [sb(f"expert_hot{k}", [P, NT, NE]) for k in range(2)]
        OH = sb("expert_hot", [P, NT, NE])
        tot, pos = sb("tile_totals", [P, NT, NE]), sb("position", [P, NT, NE])
        before = sb("tile_before", [P, NT + 1, NE])
        nblk, bend, bfirst, ones32 = sb("blocks", [P, NE]), sb("block_end", [P, NE]), sb("first_slot", [P, NE]), sb("ones32", [P, NE])
        cmp16, cmpb = sb("count_cmp", [P, NE, NT]), sb("block_cmp", [1, NBT, NE])
        iota_i, iota_f = sb("iota_i", [P, P], I32), sb("iota_f", [P, P])
        tok_i, tok = sb("token_i", [P, NT], I32), sb("token_f", [P, NT])
        dest = sb("dest_f", [P, NT])
        row_i, blk_i = sb("row_i", [P, NT], I32), sb("blk_i", [P, NT], I32)
        row, blk = sb("row_f", [P, NT]), sb("blk_f", [P, NT])
        rowhot = [sb(f"row_hot{k}", [P, NT, P]) for k in range(2)]
        blkhot = [sb(f"blk_hot{k}", [P, NT, NB]) for k in range(2)]
        ebf = sb("block_expert_f", [1, NBT])
        pR, pC, pS = ps("rank_ps", [P, NT * NE]), ps("total_ps", [P, NT * NE]), ps("slot_ps", [P, NB])
        const, chain, exps, counted, slotted = (sem(n) for n in ("route_const", "chain", "route_exp", "counted", "slotted"))
        asked_exp = sem("asked_exp")

        block = ctx.enter_context(nc.Block())
        lg = m.logits[:].rearrange("p (t e) -> p t e", e=NR)

        @block.gpsimd
        def _(pool):
            pool.iota(iota_i[:], [[1, P]], base=0, channel_multiplier=0).then_inc(const, 1)
            pool.iota(tok_i[:], [[P, NT]], base=0, channel_multiplier=1).then_inc(const, 1)
            pool.memset(ones32[:], 1.0).then_inc(const, 1)
            pool.memset(before[:, 0, :], 0.0).then_inc(const, 1)
            pool.memset(m.slot_token[:], 0).then_inc(const, 1)

        @block.scalar
        def _(act):
            act.wait_ge(asked_exp, 1)
            act.activation(gx[:], gx[:], ACT.Exp).then_inc(exps, 1)
            act.wait_ge(asked_exp, 2)
            act.activation(e21[:], e21[:], ACT.Exp).then_inc(exps, 1)

        @block.tensor
        def _(pe):
            pe.wait_ge(counted, 1)
            pe.matmul(pR[:], m.upper[:], OH[:].rearrange("p t e -> p (t e)"), start=True, stop=True)
            pe.matmul(pC[:], m.ones[:], OH[:].rearrange("p t e -> p (t e)"), start=True, stop=True).then_inc(counted, 1)
            pe.wait_ge(slotted, 1)
            for n in range(2 * NT):
                last = pe.matmul(pS[:], rowhot[n // NT][:, n % NT], blkhot[n // NT][:, n % NT], start=(n == 0), stop=(n == 2 * NT - 1))
            last.then_inc(slotted, 1)

        @block.vector
        def _(dve):
            n = [0]

            def do(ins):
                n[0] += 1
                ins.then_inc(chain, 1)
                dve.wait_ge(chain, n[0])

            def over(ap, k):
                return ap.unsqueeze(2).to_broadcast([P, NT, k])

            def first_of(dst, src, best, k):
                order = iota_f[:, 0:k].unsqueeze(1).to_broadcast([P, NT, k])
                do(dve.tensor_tensor(dst, src, over(best, k), ALU.is_ge))
                do(dve.scalar_tensor_tensor(out=tmp[:, :, 0:k], in0=order, scalar=-float(k), in1=dst, op0=ALU.add, op1=ALU.mult))
                do(dve.tensor_reduce(first[:], tmp[:, :, 0:k], AX.X, ALU.min))
                do(dve.tensor_tensor(tmp[:, :, 0:k], tmp[:, :, 0:k], over(first[:], k), ALU.is_equal))
                do(dve.tensor_tensor(dst, dst, tmp[:, :, 0:k], ALU.mult))

            dve.wait_ge(const, 5)
            do(dve.tensor_copy(iota_f[:], iota_i[:]))
            do(dve.tensor_copy(tok[:], tok_i[:]))
            g = lg[:, :, 0:NG]
            do(dve.tensor_reduce(gmax[:], g, AX.X, ALU.max))
            dve.tensor_tensor(gx[:], g, over(gmax[:], NG), ALU.subtract).then_inc(asked_exp, 1)
            first_of(gh[:], g, gmax[:], NG)
            dve.wait_ge(exps, 1)
            do(dve.tensor_reduce(gsum[:], gx[:], AX.X, ALU.add))
            do(dve.reciprocal(pg[:], gsum[:]))
            do(dve.tensor_tensor(prod[:], lg[:, :, NG:].rearrange("p t (g e) -> p t g e", g=NG),
                                 gh[:].unsqueeze(3).to_broadcast([P, NT, NG, EG]), ALU.mult))
            do(dve.tensor_reduce(le[:], prod[:].rearrange("p t g e -> p t e g"), AX.X, ALU.add))
            do(dve.tensor_reduce(top[0][:], le[:], AX.X, ALU.max))
            first_of(hot[0][:], le[:], top[0][:], EG)
            do(dve.scalar_tensor_tensor(out=le[:], in0=hot[0][:], scalar=NEG, in1=le[:], op0=ALU.mult, op1=ALU.add))
            do(dve.tensor_reduce(top[1][:], le[:], AX.X, ALU.max))
            dve.tensor_tensor(e21[:], top[1][:], top[0][:], ALU.subtract).then_inc(asked_exp, 1)
            first_of(hot[1][:], le[:], top[1][:], EG)
            for k in range(2):
                do(dve.tensor_tensor(E[k][:].rearrange("p t (g e) -> p t g e", g=NG), gh[:].unsqueeze(3).to_broadcast([P, NT, NG, EG]),
                                     hot[k][:].unsqueeze(2).to_broadcast([P, NT, NG, EG]), ALU.mult))
            dve.tensor_tensor(OH[:], E[0][:], E[1][:], ALU.add).then_inc(counted, 1)
            dve.wait_ge(exps, 2)
            do(dve.tensor_scalar(den[:], e21[:], 1.0, None, ALU.add))
            do(dve.reciprocal(den[:], den[:]))
            do(dve.tensor_tensor(m.gates[:, 0], den[:], pg[:], ALU.mult))
            do(dve.tensor_tensor(m.gates[:, 1], m.gates[:, 0], e21[:], ALU.mult))
            dve.wait_ge(counted, 2)
            do(dve.tensor_copy(tot[:].rearrange("p t e -> p (t e)"), pC[:]))
            for t in range(NT):
                do(dve.tensor_tensor(before[:, t + 1], before[:, t], tot[:, t], ALU.add))
            do(dve.tensor_tensor(pos[:], pR[:].rearrange("p (t e) -> p t e", e=NE), before[:, 0:NT], ALU.add))
            steps_ = iota_f[:, 0:NT].unsqueeze(1).to_broadcast([P, NE, NT])
            do(dve.tensor_copy(cmp16[:], steps_))
            do(dve.scalar_tensor_tensor(out=cmp16[:], in0=cmp16[:], scalar=float(P),
                                        in1=before[:, NT].unsqueeze(2).to_broadcast([P, NE, NT]), op0=ALU.mult, op1=ALU.is_lt))
            do(dve.tensor_reduce(nblk[:], cmp16[:], AX.X, ALU.add))
            do(dve.tensor_tensor_scan(bend[:], ones32[:], nblk[:], 0.0, ALU.mult, ALU.add))
            do(dve.tensor_tensor(bfirst[:], bend[:], nblk[:], ALU.subtract))
            do(dve.tensor_scalar(bfirst[:], bfirst[:], float(P), -1.0, ALU.mult, ALU.add))
            do(dve.tensor_tensor(pos[:], pos[:], bfirst[:].unsqueeze(1).to_broadcast([P, NT, NE]), ALU.add))
            for k in range(2):
                do(dve.tensor_tensor(E[k][:], E[k][:], pos[:], ALU.mult))
                do(dve.tensor_reduce(dest[:], E[k][:], AX.X, ALU.add))
                do(dve.tensor_copy(m.dest[:, k], dest[:]))
                do(dve.tensor_scalar(row_i[:], m.dest[:, k], P - 1, None, ALU.bitwise_and))
                do(dve.tensor_scalar(blk_i[:], m.dest[:, k], P.bit_length() - 1, None, ALU.logical_shift_right))
                do(dve.tensor_copy(row[:], row_i[:]))
                do(dve.tensor_copy(blk[:], blk_i[:]))
                do(dve.tensor_tensor(rowhot[k][:], iota_f[:].unsqueeze(1).to_broadcast([P, NT, P]), over(row[:], P), ALU.is_equal))
                do(dve.tensor_tensor(blkhot[k][:], iota_f[:, 0:NB].unsqueeze(1).to_broadcast([P, NT, NB]), over(blk[:], NB), ALU.is_equal))
                ins = dve.tensor_tensor(blkhot[k][:], blkhot[k][:], over(tok[:], NB), ALU.mult)
                if k == 0:
                    do(ins)
                else:
                    ins.then_inc(slotted, 1)
            do(dve.tensor_tensor(cmpb[:], iota_f[0:1, 0:NBT].unsqueeze(2).to_broadcast([1, NBT, NE]),
                                 bend[0:1].unsqueeze(1).to_broadcast([1, NBT, NE]), ALU.is_ge))
            do(dve.tensor_reduce(ebf[:], cmpb[:], AX.X, ALU.add))
            do(dve.tensor_scalar(ebf[:], ebf[:], float(NE - 1), None, ALU.min))
            do(dve.tensor_copy(m.block_expert[:], ebf[:]))
            do(dve.tensor_scalar(m.block_slot[:], m.block_expert[:], WSLOTS - 1, None, ALU.bitwise_and))
            do(dve.tensor_copy(m.block_end[:, 0:NE], bend[0:1]))
            do(dve.tensor_scalar(m.block_end[:, NE:NE + 1], m.block_end[:, NE - 1:NE], 1, None, ALU.add))
            do(dve.tensor_scalar(m.block_end[:, NE:NE + 1], m.block_end[:, NE:NE + 1], 1, None, ALU.logical_shift_right))
            dve.wait_ge(slotted, 2)
            do(dve.tensor_copy(m.slot_token[:, 0:NB], pS[:]))


def experts(nc, m, w1, w3, w2):
    with nc.cleanup_on_exit(), ExitStack() as ctx:
        sb = lambda n, s, d=F32: ctx.enter_context(nc.sbuf_tensor(n, s, d))
        ps = lambda n, s: ctx.enter_context(nc.psum_tensor(n, s, F32))
        sems = []

        def sem(name):
            sems.append(nc.alloc_semaphore(name))
            return sems[-1]

        idx = [sb(f"row_index{i}", [P, 1], I32) for i in range(2)]
        hg = [sb(f"h_rows{i}", [P, D]) for i in range(2)]
        xT = [sb(f"h_rowsT{i}", [P, ND, P]) for i in range(2)]
        act_, hid = sb("silu_gate", [P, 2, DE]), sb("hidden", [P, 2, DE])
        hT = [sb(f"hiddenT{i}", [P, 2, P]) for i in range(2)]
        y = sb("expert_y", [P, 2, D])
        pX, pH, pHT, pY = ps("rowsT_ps", [P, 2, 512]), [ps(f"hidden_ps{i}", [P, 512]) for i in range(2)], ps(
            "hiddenT_ps", [P, 2, P]), ps("expert_ps", [P, 2, 512])
        wait_point, idx_copied, weights_ready = sem("wait_point6"), sem("idx_copied"), sem("weights_ready")
        gathered = [nc.alloc_semaphore(f"gathered{i}") for i in range(2)]
        xT_ready, xT_act, xT_dve = sem("xT_ready6"), sem("xT_act6"), sem("xT_dve6")
        up_ready, silu_ready, hid_ready = sem("up_ready"), sem("silu_ready"), sem("hid_ready")
        hT_ready, hT_copied, down_ready = sem("hT_ready6"), sem("hT_copied6"), sem("down_ready")
        y_act, y_dve = sem("y_act6"), sem("y_dve6")
        y_stored = [sem(f"y_stored6_{i}") for i in range(2)]

        def pairs(eng):
            return eng.value_load(m.block_end[0:1, NE:NE + 1], min_val=1, max_val=NB // 2)

        def waiter(eng, held=False):
            def wait(q, v):
                if isinstance(v, int):
                    if v > 0:
                        eng.wait_ge(q, START + v)
                elif held:
                    held_wait(eng, q, v, wait_point)
                else:
                    eng.wait_ge(q, START + v)
            return wait

        block = ctx.enter_context(nc.Block())

        @block.sync
        def _(sp):
            start_counts(sp, sems[0::5])
            for e in range(WSLOTS):
                sp.wait_ge(m.expert_loaded[e], START + 48)
                sp.sem_inc(weights_ready, 1)
            with sp.Fori(1, NE // WSLOTS) as i:
                for s in range(WSLOTS):
                    e = i * WSLOTS + s
                    end = sp.value_load(m.block_end[0:1, ds(e - WSLOTS, 1)], min_val=0, max_val=NB)
                    held_wait(sp, down_ready, end, wait_point)
                    load_expert(sp, m, w1, w3, w2, e, s)
                    if s:
                        held_wait(sp, m.expert_loaded[s - 1], i * 48 + 48, wait_point)
                        sp.sem_inc(weights_ready, 1)
                held_wait(sp, m.expert_loaded[WSLOTS - 1], i * 48 + 48, wait_point)
                sp.sem_inc(weights_ready, 1)

        @block.gpsimd
        def _(pool):
            start_counts(pool, sems[1::5])
            wait = waiter(pool, True)

            def gather(b, par):
                wait(gathered[par], (b - par) * 8 - START)
                pool.tensor_copy(idx[par][:], m.slot_token[:, ds(b, 1)]).then_inc(idx_copied, 1)
                wait(idx_copied, b + 1)
                wait(xT_ready, b - 1)
                pool.indirect_dma_start(hg[par][:], None, m.h2_d, bass.IndirectOffsetOnAxis(ap=idx[par][:, 0:1], axis=0)
                                        ).then_inc(gathered[par], 16)

            n = pairs(pool)
            gather(0, 0)
            gather(1, 1)
            with pool.Fori(0, n) as i:
                gather(i * 2 + 2, 0)
                gather(i * 2 + 3, 1)
            wait(gathered[0], n * 16 + 16 - START)
            wait(gathered[1], n * 16 + 16 - START)

        @block.scalar
        def _(act):
            start_counts(act, sems[2::5])
            wait = waiter(act)

            def rows(b, par):
                wait(xT_ready, b + 1)
                wait(up_ready, b - 1)
                act.copy(xT[par][:, 0:4].rearrange("p k t -> p (k t)"), pX[:, 0]).then_inc(xT_act, 1)

            def silu(b, par):
                wait(up_ready, b + 1)
                act.activation(act_[:, par], pH[par][:, 0:DE], ACT.Silu).then_inc(silu_ready, 1)

            def body(b, par):
                silu(b + 1, 1 - par)
                wait(hT_ready, b + 1)
                act.copy(hT[par][:], pHT[:]).then_inc(hT_copied, 1)
                rows(b + 2, par)
                wait(down_ready, b + 1)
                wait(y_stored[par], (b - par) * 8)
                act.copy(y[:, par, 0:512], pY[:, 0]).then_inc(y_act, 1)
                wait(y_act, b + 1)
                wait(y_dve, b + 1)
                act.sem_inc(wait_point, 1)
                act.dma_start(m.ys_d[ds(b * P, P), :], y[:, par]).then_inc(y_stored[par], 16)

            n = pairs(act)
            rows(0, 0)
            rows(1, 1)
            silu(0, 0)
            with act.Fori(0, n) as i:
                body(i * 2, 0)
                body(i * 2 + 1, 1)
            for p in range(2):
                held_wait(act, y_stored[p], n * 16, wait_point)

        @block.vector
        def _(dve):
            start_counts(dve, sems[3::5])
            wait = waiter(dve)

            def rows(b, par):
                wait(xT_ready, b + 1)
                wait(up_ready, b - 1)
                dve.tensor_copy(xT[par][:, 4:8].rearrange("p k t -> p (k t)"), pX[:, 1]).then_inc(xT_dve, 1)

            def hidden(b, par):
                wait(silu_ready, b + 1)
                wait(hT_ready, b - 1)
                dve.tensor_tensor(hid[:, par], act_[:, par], pH[par][:, DE:], ALU.mult).then_inc(hid_ready, 1)

            def body(b, par):
                hidden(b + 1, 1 - par)
                rows(b + 2, par)
                wait(down_ready, b + 1)
                wait(y_stored[par], (b - par) * 8)
                dve.tensor_copy(y[:, par, 512:], pY[:, 1]).then_inc(y_dve, 1)

            n = pairs(dve)
            rows(0, 0)
            rows(1, 1)
            hidden(0, 0)
            with dve.Fori(0, n) as i:
                body(i * 2, 0)
                body(i * 2 + 1, 1)

        @block.tensor
        def _(pe):
            start_counts(pe, sems[4::5])
            wait = waiter(pe)

            def rows(b, par):
                wait(gathered[par], (b - par) * 8 + 16 - START)
                wait(xT_act, b)
                wait(xT_dve, b)
                for k in range(ND):
                    last = pe.transpose(pX[:, k // 4, (k % 4) * P:(k % 4 + 1) * P], hg[par][:, k * P:(k + 1) * P], m.ident[:])
                last.then_inc(xT_ready, 1)

            def up(b, par):
                expert = pe.value_load(m.block_expert[0:1, ds(b, 1)], min_val=0, max_val=NE - 1)
                slot = pe.value_load(m.block_slot[0:1, ds(b, 1)], min_val=0, max_val=WSLOTS - 1)
                wait(weights_ready, expert + 1)
                wait(xT_act, b + 1)
                wait(xT_dve, b + 1)
                wait(hid_ready, b - 1)
                for k in range(ND):
                    last = pe.matmul(pH[par][:], xT[par][:, k], m.w13[:, ds(slot, 1), k].rearrange("p s n -> p (s n)"),
                                     start=(k == 0), stop=(k == ND - 1))
                last.then_inc(up_ready, 1)

            def down(b, par):
                slot = pe.value_load(m.block_slot[0:1, ds(b, 1)], min_val=0, max_val=WSLOTS - 1)
                wait(hT_copied, b + 1)
                wait(y_act, b)
                wait(y_dve, b)
                for half in range(2):
                    for k in range(2):
                        last = pe.matmul(pY[:, half], hT[par][:, k],
                                         m.w2b[:, ds(slot, 1), k, half * 512:(half + 1) * 512].rearrange("p s n -> p (s n)"),
                                         start=(k == 0), stop=(k == 1))
                last.then_inc(down_ready, 1)

            def body(b, par):
                up(b + 1, 1 - par)
                wait(hid_ready, b + 1)
                wait(hT_copied, b)
                for k in range(2):
                    last = pe.transpose(pHT[:, k], hid[:, par, k * P:(k + 1) * P], m.ident[:])
                last.then_inc(hT_ready, 1)
                rows(b + 2, par)
                down(b, par)

            n = pairs(pe)
            rows(0, 0)
            rows(1, 1)
            up(0, 0)
            with pe.Fori(0, n) as i:
                body(i * 2, 0)
                body(i * 2 + 1, 1)


def combine(nc, m, final_norm, out):
    with nc.cleanup_on_exit(), ExitStack() as ctx:
        sb = lambda n, s, d=F32: ctx.enter_context(nc.sbuf_tensor(n, s, d))
        sem = nc.alloc_semaphore
        DEPTH = 4
        fgain = sb("final_gain", [P, D])
        ya, yb, xr = sb("rows_a", [P, DEPTH, D]), sb("rows_b", [P, DEPTH, D]), sb("x1_in", [P, DEPTH, D])
        s0, s1, x2, ob, junk = sb("gated_a", [P, 2, D]), sb("gated_sum", [P, D]), sb("x2", [P, 2, D]), sb("out_tile", [P, 2, D]), sb("junk7", [P, D])
        ss, ms, rs = sb("x2_sumsq", [P, 2]), sb("x2_meansq", [P, 2]), sb("x2_rstd", [P, 2])
        gain_loaded = sem("gain_loaded")
        x_loaded, y_loaded = [sem(f"x_loaded7_{i}") for i in range(DEPTH)], [sem(f"y_loaded7_{i}") for i in range(DEPTH)]
        a_gated, sum_step, x2_ready, squared, powed, out_ready = (sem(n) for n in (
            "a_gated", "sum_step", "x2_ready", "squared7", "powed7", "out_ready7"))
        stored = [sem(f"stored7_{i}") for i in range(2)]
        block = ctx.enter_context(nc.Block())

        @block.sync
        def _(sp):
            sp.dma_start(fgain[:], final_norm.rearrange("(a n) -> a n", a=1).partition_broadcast(P)).then_inc(gain_loaded, 16)
            for t in range(DEPTH):
                sp.dma_start(xr[:, t], m.x1_d[t * P:(t + 1) * P, :]).then_inc(x_loaded[t], 16)
            for t in range(NT):
                sp.wait_ge(out_ready, t + 1)
                sp.dma_start(out[0, t * P:(t + 1) * P, :], ob[:, t % 2]).then_inc(stored[t % 2], 16)
                if t + DEPTH < NT:
                    sp.dma_start(xr[:, t % DEPTH], m.x1_d[(t + DEPTH) * P:(t + DEPTH + 1) * P, :]).then_inc(x_loaded[t % DEPTH], 16)
            for i in range(2):
                sp.wait_ge(stored[i], 16 * NT // 2)

        @block.gpsimd
        def _(pool):
            def gather(t):
                for k, dst in enumerate((ya, yb)):
                    pool.indirect_dma_start(dst[:, t % DEPTH], None, m.ys_d,
                                            bass.IndirectOffsetOnAxis(ap=m.dest[:, k, t:t + 1], axis=0)).then_inc(y_loaded[t % DEPTH], 16)

            for t in range(DEPTH):
                gather(t)
            for t in range(NT):
                b = t % 2
                pool.wait_ge(sum_step, 2 * t + 2)
                pool.wait_ge(x_loaded[t % DEPTH], 16 * (t // DEPTH + 1))
                if t >= 2:
                    pool.wait_ge(out_ready, t - 1)
                pool.tensor_tensor(x2[:, b], s1[:], xr[:, t % DEPTH], ALU.add).then_inc(x2_ready, 1)
                if t + DEPTH < NT:
                    gather(t + DEPTH)
                pool.wait_ge(squared, t + 1)
                pool.tensor_scalar(ms[:, b:b + 1], ss[:, b:b + 1], 1.0 / D, EPS, ALU.mult, ALU.add).then_inc(powed, 1)
                pool.wait_ge(powed, 2 * t + 1)
                pool.tensor_tensor(rs[:, b:b + 1], ms[:, b:b + 1], m.half_pow[:, 0:1], ALU.pow).then_inc(powed, 1)

        @block.scalar
        def _(act):
            def gated(t):
                act.wait_ge(y_loaded[t % DEPTH], 32 * (t // DEPTH + 1))
                if t >= 2:
                    act.wait_ge(sum_step, 2 * t - 3)
                act.activation(s0[:, t % 2], ya[:, t % DEPTH], ACT.Copy, scale=m.gates[:, 0, t:t + 1]).then_inc(a_gated, 1)

            gated(0)
            for t in range(NT):
                if t + 1 < NT:
                    gated(t + 1)
                act.wait_ge(x2_ready, t + 1)
                if t >= 2:
                    act.wait_ge(powed, 2 * t - 3)
                act.activation(junk[:], x2[:, t % 2], ACT.Square, accum_out=ss[:, t % 2:t % 2 + 1]).then_inc(squared, 1)

        @block.vector
        def _(dve):
            dve.wait_ge(gain_loaded, 16)

            def summed(t):
                dve.wait_ge(a_gated, t + 1)
                dve.wait_ge(y_loaded[t % DEPTH], 32 * (t // DEPTH + 1))
                if t:
                    dve.wait_ge(x2_ready, t)
                dve.scalar_tensor_tensor(out=s1[:], in0=yb[:, t % DEPTH], scalar=m.gates[:, 1, t:t + 1], in1=s0[:, t % 2],
                                         op0=ALU.mult, op1=ALU.add).then_inc(sum_step, 1)
                dve.wait_ge(sum_step, 2 * t + 1)
                dve.tensor_tensor(s1[:], s1[:], m.gate_m, ALU.mult).then_inc(sum_step, 1)

            summed(0)
            for t in range(NT):
                if t + 1 < NT:
                    summed(t + 1)
                dve.wait_ge(powed, 2 * t + 2)
                if t >= 2:
                    dve.wait_ge(stored[t % 2], 16 * (t // 2))
                dve.scalar_tensor_tensor(out=ob[:, t % 2], in0=x2[:, t % 2], scalar=rs[:, t % 2:t % 2 + 1], in1=fgain[:],
                                         op0=ALU.mult, op1=ALU.mult).then_inc(out_ready, 1)


def trunk(nc, x, c, positions, w_mod, b_mod, attn_norm, w_in, q_norm, w_uq, kv_norm, w_ukv, conv_w, a_log, dt_bias,
          mla_out_norm, gdn_out_norm, w_out, moe_norm, w_route_group, b_route_group, w_route_expert, b_route_expert,
          w1, w3, w2, final_norm, out):
    with ExitStack() as ctx:
        sb = lambda n, s, d=F32: ctx.enter_context(nc.sbuf_tensor(n, s, d))
        dram = lambda n, s, d=F32: nc.dram_tensor(n, s, d, kind="Internal").ap()
        ctx.enter_context(nc.allow_non_contiguous_dma(reason="vectors of a few KiB, to columns"))
        m = Shared()
        m.ident, m.ones, m.upper = sb("ident", [P, P]), sb("ones", [P, P]), sb("upper", [P, P])
        m.eps, m.half_pow = sb("eps", [P, 1]), sb("half_pow", [P, 32])
        m.shift_a, m.gain_a = sb("shift_a", [P, ND]), sb("gain_a", [P, ND])
        m.c_act, m.mod_rows = sb("c_act", [P, ND]), sb("mod_rows", [P, 4, D])
        m.gate_a, m.shift_m, m.gain_m, m.gate_m = (m.mod_rows[:, part] for part in range(4))
        m.sin, m.cos = sb("rope_sin", [P, NT * HALF]), sb("rope_cos", [P, NT * HALF])
        m.ab = sb("decay_beta", [P, NT * 2 * GH])
        m.gate_d, m.v_d = dram("gate_d", [T, GH * GD]), dram("v_d", [T, AH * DV])
        m.qT_d, m.kT_d = dram("qT_d", [NT * QK, AH * P]), dram("kT_d", [NT * QK, AH * P])
        m.qkv_d = dram("qkv_d", [NT, P, NC, P])
        m.y_d = dram("y_d", [T, D])
        m.win_loaded = ctx.enter_context(nc.semaphore("win_loaded"))
        with nc.sbuf_tensor("w_in_sb", [P, ND, DIN], F32) as m.win:
            modulation(nc, m, c, positions, w_mod, b_mod, attn_norm, w_in)
            projection(nc, m, x, q_norm, w_uq, kv_norm, w_ukv, conv_w)
        delta(nc, m, a_log, dt_bias, w_mod, b_mod)
        m.ys_d = dram("ys_d", [NB * P, D])
        attention(nc, m)
        m.x1_d, m.h2_d = dram("x1_d", [T, D]), dram("h2_d", [T, D])
        m.logits = sb("logits", [P, NT * (NG + NE)])
        m.gates, m.dest = sb("gates", [P, 2, NT]), sb("dest", [P, 2, NT], I32)
        m.slot_token = sb("slot_token", [P, NBT], I32)
        m.block_expert, m.block_slot = sb("block_expert", [1, NBT], I32), sb("block_slot", [1, NBT], I32)
        m.block_end = sb("block_end_i", [1, NE + 1], I32)
        m.w13, m.w2b = sb("w13", [P, WSLOTS, ND, 2 * DE]), sb("w2_sb", [P, WSLOTS, 2, D])
        m.expert_loaded = [ctx.enter_context(nc.semaphore(f"expert_loaded{i}")) for i in range(WSLOTS)]
        output(nc, m, x, mla_out_norm, gdn_out_norm, w_out, w_route_group, b_route_group, w_route_expert, b_route_expert,
               moe_norm, w1, w3, w2)
        routing(nc, m)
        experts(nc, m, w1, w3, w2)
        combine(nc, m, final_norm, out)


_INS = ['x', 'c', 'positions', 'w_mod', 'b_mod', 'attn_norm', 'w_in', 'q_norm', 'w_uq', 'kv_norm', 'w_ukv', 'conv_w',
        'a_log', 'dt_bias', 'mla_out_norm', 'gdn_out_norm', 'w_out', 'moe_norm', 'w_route_group', 'b_route_group',
        'w_route_expert', 'b_route_expert', 'w1', 'w3', 'w2', 'final_norm']
_OUTS = [((1, 2048, 1024), 'float32')]


def kernel(**inputs):
    import numpy as _np
    import concourse.bacc as _bacc
    from concourse import mybir as _mybir
    from concourse.bass_utils import run_bass_kernel_spmd as _run

    nc = _bacc.Bacc("TRN2", target_bir_lowering=False, num_devices=1)
    arrays, args = {}, []
    for name in _INS:
        a = _np.ascontiguousarray(inputs[name])
        arrays[f"in_{name}_dram"] = a
        args.append(nc.dram_tensor(f"in_{name}_dram", a.shape, _mybir.dt.from_np(a.dtype), kind="ExternalInput").ap())
    for i, (shape, dtype) in enumerate(_OUTS):
        dt = _mybir.dt.from_np(_np.dtype(dtype))
        args.append(nc.dram_tensor(f"out_{i}_dram", shape, dt, kind="ExternalOutput").ap())
    trunk(nc, *args)
    r = _run(nc, [arrays], core_ids=[0])
    got = tuple(r.results[0][f"out_{i}_dram"] for i in range(len(_OUTS)))
    return got[0]
```
